# Optimizing a Trainium2 kernel written in Bass

```python
import jax, jax.numpy as jnp
from jax import lax
import numpy as np

D_MODEL = 1024
BATCH = 1
SEQ = 256
DEPTH = 2

RMS_EPS = 1e-6
L2_EPS = 1e-6
NEG_INF = -1e30

DN_HEADS = 4
DN_HEAD_DIM = 128
DN_WIDTH = DN_HEADS * DN_HEAD_DIM
DN_CONV = 4
DN_CHUNK = 64

SC_GROUPS = 4
SC_WIDTH = SC_GROUPS * 128
SC_CONV = 3

SWA_Q_HEADS = 16
SWA_KV_HEADS = 2
SWA_HEAD_DIM = 64
SWA_WINDOW = 128
SWA_BLOCK = 128

FFN_DIM = 3584
N_EXPERTS = 8
TOP_K = 2
EXPERT_DIM = 3584

EVEN_IN_SIZES = (DN_WIDTH, DN_WIDTH, DN_WIDTH,
                 DN_WIDTH,
                 DN_HEADS, DN_HEADS,
                 SC_WIDTH, SC_WIDTH, SC_WIDTH)
EVEN_IN = sum(EVEN_IN_SIZES)
EVEN_MIX = DN_WIDTH + SC_WIDTH
ODD_IN_SIZES = (SWA_Q_HEADS * SWA_HEAD_DIM, SWA_KV_HEADS * SWA_HEAD_DIM, SWA_KV_HEADS * SWA_HEAD_DIM)
ODD_IN = sum(ODD_IN_SIZES)
ODD_MIX = SWA_Q_HEADS * SWA_HEAD_DIM

kernel_name = "hybrid_deltanet_shortconv_swa_moe"

def rms_norm(x, w):
    xf = x.astype(jnp.float32)
    y = xf * lax.rsqrt(jnp.mean(xf * xf, axis=-1, keepdims=True) + RMS_EPS)
    return (y * w.astype(jnp.float32)).astype(x.dtype)

def l2_norm(x):
    xf = x.astype(jnp.float32)
    return xf * lax.rsqrt(jnp.sum(xf * xf, axis=-1, keepdims=True) + L2_EPS)

def split_cols(t, sizes):
    offs = np.cumsum(sizes)[:-1].tolist()
    return jnp.split(t, offs, axis=-1)

def causal_depthwise_conv(x, w):
    width, ch = w.shape
    return lax.conv_general_dilated(
        x, w[:, None, :].astype(x.dtype), window_strides=(1,),
        padding=[(width - 1, 0)], dimension_numbers=('NWC', 'WIO', 'NWC'),
        feature_group_count=ch)

def gated_delta_rule(q, k, v, g, beta):
    bsz, seqlen, nh, dk = q.shape
    dv = v.shape[-1]
    c = DN_CHUNK
    nc = seqlen // c

    def chunks(t):
        t = t.astype(jnp.float32).reshape((bsz, nc, c, nh) + t.shape[3:])
        return jnp.moveaxis(t, 3, 1)

    q, k, v, g, beta = (chunks(t) for t in (q, k, v, g, beta))
    q = q * (dk ** -0.5)
    g_cum = jnp.cumsum(g, axis=-1)
    causal = jnp.tril(jnp.ones((c, c), dtype=bool))
    strict = jnp.tril(jnp.ones((c, c), dtype=bool), k=-1)
    diff = g_cum[..., :, None] - g_cum[..., None, :]
    decay = jnp.where(causal, jnp.exp(jnp.where(causal, diff, 0.0)), 0.0)
    k_beta = k * beta[..., None]
    v_beta = v * beta[..., None]
    lower = jnp.where(strict, jnp.einsum('bhnid,bhnjd->bhnij', k_beta, k) * decay, 0.0)
    eye = jnp.broadcast_to(jnp.eye(c, dtype=jnp.float32), lower.shape)
    t_inv = lax.linalg.triangular_solve(lower, eye, left_side=True, lower=True,
                                        unit_diagonal=True)
    u = jnp.einsum('bhnij,bhnjd->bhnid', t_inv, v_beta)
    w = jnp.einsum('bhnij,bhnjd->bhnid', t_inv, k_beta * jnp.exp(g_cum)[..., None])
    q_dec = q * jnp.exp(g_cum)[..., None]
    attn = jnp.einsum('bhnid,bhnjd->bhnij', q, k) * decay
    k_dec = k * jnp.exp(g_cum[..., -1:] - g_cum)[..., None]
    g_end = jnp.exp(g_cum[..., -1])

    def step(state, xs):
        q_n, w_n, u_n, a_n, kd_n, ge_n = xs
        v_new = u_n - jnp.einsum('bhcd,bhde->bhce', w_n, state)
        o_n = (jnp.einsum('bhcd,bhde->bhce', q_n, state)
               + jnp.einsum('bhij,bhje->bhie', a_n, v_new))
        state = state * ge_n[..., None, None] + jnp.einsum('bhcd,bhce->bhde', kd_n, v_new)
        return state, o_n

    xs = tuple(jnp.moveaxis(t, 2, 0) for t in (q_dec, w, u, attn, k_dec, g_end))
    s0 = jnp.zeros((bsz, nh, dk, dv), jnp.float32)
    _, o = lax.scan(step, s0, xs)
    return jnp.transpose(o, (1, 0, 3, 2, 4)).reshape(bsz, seqlen, nh, dv)

def even_mixer(h, w_in, conv_qkv, a_log, dt_bias, o_norm, conv_sc, w_out):
    bsz, seqlen, _ = h.shape
    proj = jnp.einsum('bsd,de->bse', h, w_in)
    q, k, v, z, a, b, bg, cg, xin = split_cols(proj, EVEN_IN_SIZES)
    qkv = jax.nn.silu(causal_depthwise_conv(jnp.concatenate([q, k, v], axis=-1), conv_qkv))
    q, k, v = jnp.split(qkv, 3, axis=-1)
    hs = (bsz, seqlen, DN_HEADS, DN_HEAD_DIM)
    q = l2_norm(q.reshape(hs))
    k = l2_norm(k.reshape(hs))
    v = v.reshape(hs)
    beta = jax.nn.sigmoid(b.astype(jnp.float32))
    g = -jnp.exp(a_log.astype(jnp.float32)) * jax.nn.softplus(
        a.astype(jnp.float32) + dt_bias.astype(jnp.float32))
    o = gated_delta_rule(q, k, v, g, beta)
    o = rms_norm(o, o_norm) * jax.nn.silu(z.astype(jnp.float32).reshape(hs))
    o = o.reshape(bsz, seqlen, DN_WIDTH).astype(h.dtype)
    y_sc = bg * causal_depthwise_conv(cg * xin, conv_sc)
    mix = jnp.concatenate([o, y_sc], axis=-1)
    return jnp.einsum('bse,ed->bsd', mix, w_out)

def sliding_window_attention(q, k, v, sinks):
    bsz, seqlen, nq, hd = q.shape
    nkv = k.shape[2]
    grp = nq // nkv
    blk = SWA_BLOCK
    nb = seqlen // blk
    qb = q.reshape(bsz, nb, blk, nkv, grp, hd)
    pad = ((0, 0), (blk, 0), (0, 0), (0, 0))
    kp = jnp.pad(k, pad).reshape(bsz, nb + 1, blk, nkv, hd)
    vp = jnp.pad(v, pad).reshape(bsz, nb + 1, blk, nkv, hd)
    kw = jnp.concatenate([kp[:, :-1], kp[:, 1:]], axis=2)
    vw = jnp.concatenate([vp[:, :-1], vp[:, 1:]], axis=2)
    sink = sinks.astype(jnp.float32).reshape(nkv, grp)[None, :, :, None, None]
    qpos = jnp.arange(blk)[:, None] + blk
    kpos = jnp.arange(2 * blk)[None, :]
    rel = qpos - kpos
    band = (rel >= 0) & (rel < SWA_WINDOW)
    scale = hd ** -0.5

    def block(args):
        n, qn, kn, vn = args
        s = jnp.einsum('bqhgd,bkhd->bhgqk', qn, kn).astype(jnp.float32) * scale
        valid = band & (kpos + (n - 1) * blk >= 0)
        s = jnp.where(valid, s, NEG_INF)
        m = jnp.maximum(jnp.max(s, axis=-1, keepdims=True), sink)
        p = jnp.exp(s - m)
        denom = jnp.sum(p, axis=-1, keepdims=True) + jnp.exp(sink - m)
        pr = (p / denom).astype(vn.dtype)
        return jnp.einsum('bhgqk,bkhd->bqhgd', pr, vn)

    o = lax.map(block, (jnp.arange(nb), jnp.moveaxis(qb, 1, 0),
                        jnp.moveaxis(kw, 1, 0), jnp.moveaxis(vw, 1, 0)))
    return jnp.moveaxis(o, 0, 1).reshape(bsz, seqlen, nq, hd)

def odd_mixer(h, w_in, q_norm, k_norm, sinks, w_out):
    bsz, seqlen, _ = h.shape
    proj = jnp.einsum('bsd,de->bse', h, w_in)
    q, k, v = split_cols(proj, ODD_IN_SIZES)
    q = rms_norm(q.reshape(bsz, seqlen, SWA_Q_HEADS, SWA_HEAD_DIM), q_norm)
    k = rms_norm(k.reshape(bsz, seqlen, SWA_KV_HEADS, SWA_HEAD_DIM), k_norm)
    v = v.reshape(bsz, seqlen, SWA_KV_HEADS, SWA_HEAD_DIM)
    o = sliding_window_attention(q, k, v, sinks).reshape(bsz, seqlen, ODD_MIX)
    return jnp.einsum('bse,ed->bsd', o, w_out)

def swiglu(h, w1, w3, w2):
    a = jax.nn.silu(jnp.einsum('bsd,df->bsf', h, w1)) * jnp.einsum('bsd,df->bsf', h, w3)
    return jnp.einsum('bsf,fd->bsd', a, w2)

def moe_swiglu(h, w_router, w1, w3, w2):
    logits = jnp.einsum('bsd,de->bse', h, w_router).astype(jnp.float32)
    top_val, top_idx = lax.top_k(logits, TOP_K)
    top_gate = jax.nn.softmax(top_val, axis=-1)
    gates = jnp.sum(jax.nn.one_hot(top_idx, N_EXPERTS, dtype=jnp.float32)
                    * top_gate[..., None], axis=-2).astype(h.dtype)
    y = jnp.zeros_like(h)
    for e in range(N_EXPERTS):
        y = y + gates[..., e:e + 1] * swiglu(h, w1[e], w3[e], w2[e])
    return y

def setup_inputs(seed: int = 0) -> dict:
    key = jax.random.key(seed)
    ks = iter(jax.random.split(key, 32))
    f32 = jnp.float32
    ne = (DEPTH + 1) // 2
    no = DEPTH // 2

    def dense(shape, fan_in):
        return jax.random.normal(next(ks), shape, f32) * (fan_in ** -0.5)

    def gain(shape):
        return 1.0 + 0.05 * jax.random.normal(next(ks), shape, f32)

    x = jax.random.normal(next(ks), (BATCH, SEQ, D_MODEL), f32)
    a_init = jax.random.uniform(next(ks), (ne, DN_HEADS), f32, 1.0, 16.0)
    dt = jnp.exp(jax.random.uniform(next(ks), (ne, DN_HEADS), f32,
                                    float(np.log(1e-3)), float(np.log(1e-1))))
    return {
        "x": x,
        "ev_norm1": gain((ne, D_MODEL)),
        "ev_w_in": dense((ne, D_MODEL, EVEN_IN), D_MODEL),
        "ev_conv_qkv": dense((ne, DN_CONV, 3 * DN_WIDTH), DN_CONV),
        "ev_a_log": jnp.log(a_init),
        "ev_dt_bias": dt + jnp.log(-jnp.expm1(-dt)),
        "ev_o_norm": gain((ne, DN_HEAD_DIM)),
        "ev_conv_sc": dense((ne, SC_CONV, SC_WIDTH), SC_CONV),
        "ev_w_out": dense((ne, EVEN_MIX, D_MODEL), EVEN_MIX),
        "ev_norm2": gain((ne, D_MODEL)),
        "ev_ffn_w1": dense((ne, D_MODEL, FFN_DIM), D_MODEL),
        "ev_ffn_w3": dense((ne, D_MODEL, FFN_DIM), D_MODEL),
        "ev_ffn_w2": dense((ne, FFN_DIM, D_MODEL), FFN_DIM),
        "od_norm1": gain((no, D_MODEL)),
        "od_w_in": dense((no, D_MODEL, ODD_IN), D_MODEL),
        "od_q_norm": gain((no, SWA_HEAD_DIM)),
        "od_k_norm": gain((no, SWA_HEAD_DIM)),
        "od_sinks": 0.5 * jax.random.normal(next(ks), (no, SWA_Q_HEADS), f32),
        "od_w_out": dense((no, ODD_MIX, D_MODEL), ODD_MIX),
        "od_norm2": gain((no, D_MODEL)),
        "od_router": dense((no, D_MODEL, N_EXPERTS), D_MODEL),
        "od_moe_w1": dense((no, N_EXPERTS, D_MODEL, EXPERT_DIM), D_MODEL),
        "od_moe_w3": dense((no, N_EXPERTS, D_MODEL, EXPERT_DIM), D_MODEL),
        "od_moe_w2": dense((no, N_EXPERTS, EXPERT_DIM, D_MODEL), EXPERT_DIM),
    }

def reference(x, ev_norm1, ev_w_in, ev_conv_qkv, ev_a_log, ev_dt_bias, ev_o_norm,
              ev_conv_sc, ev_w_out, ev_norm2, ev_ffn_w1, ev_ffn_w3, ev_ffn_w2,
              od_norm1, od_w_in, od_q_norm, od_k_norm, od_sinks, od_w_out, od_norm2,
              od_router, od_moe_w1, od_moe_w3, od_moe_w2):
    for layer in range(DEPTH):
        i = layer // 2
        if layer % 2 == 0:
            x = x + even_mixer(rms_norm(x, ev_norm1[i]), ev_w_in[i], ev_conv_qkv[i],
                               ev_a_log[i], ev_dt_bias[i], ev_o_norm[i], ev_conv_sc[i],
                               ev_w_out[i])
            x = x + swiglu(rms_norm(x, ev_norm2[i]), ev_ffn_w1[i], ev_ffn_w3[i], ev_ffn_w2[i])
        else:
            x = x + odd_mixer(rms_norm(x, od_norm1[i]), od_w_in[i], od_q_norm[i],
                              od_k_norm[i], od_sinks[i], od_w_out[i])
            x = x + moe_swiglu(rms_norm(x, od_norm2[i]), od_router[i], od_moe_w1[i],
                               od_moe_w3[i], od_moe_w2[i])
    return x


_drawn_inputs = setup_inputs


def setup_inputs(seed=0):
    import zlib

    import numpy as np

    out = dict(_drawn_inputs(seed))
    spreads = {}
    factors = {'od_q_norm': 2.837, 'od_k_norm': 2.747, 'od_sinks': 16.594}
    for name, (base, spread) in spreads.items():
        noise = np.random.default_rng([zlib.crc32(name.encode()), seed]).standard_normal(out[name].shape)
        drawn = base * np.exp(spread * noise) if base else spread * noise
        out[name] = __import__('jax').numpy.asarray(drawn.astype(out[name].dtype))
    for name, factor in factors.items():
        out[name] = (out[name] * factor).astype(out[name].dtype)
    return out
```

```python
from contextlib import ExitStack

import numpy as np

import concourse.bass as bass
from concourse import mybir

F32 = mybir.dt.float32
F32R = mybir.dt.float32r
I32 = mybir.dt.int32
ALU = mybir.AluOpType
ACT = mybir.ActivationFunctionType
AX = mybir.AxisListType

P = 128
D = 1024
T = 256
TT = T // P
KD = D // P
H = 4
GW = 512
F = 3584
NF = F // GW
FC = GW // P
NE = 8
CAP = P
QH, KVH, HD = 16, 2, 64
GRP = QH // KVH
UNIT = KD * GW
HALF = UNIT // 2
NS = 3
EPS = 1e-6
NEG = -1e30
LEVELS = 7

U_Q, U_K, U_V, U_CG, U_XIN, U_BG, U_Z, U_OUT0, U_FFN = 0, 1, 2, 3, 4, 5, 6, 7, 9
U_IN1 = U_FFN + 3 * NF
U_OUT1 = U_IN1 + 3
U_ROUTER = U_OUT1 + 2
U_MOE = U_ROUTER + 1
U_PASS = 3 * NF * NE
EVEN_COL = {U_Q: 0, U_K: 512, U_V: 1024, U_Z: 1536, U_BG: 2056, U_CG: 2568, U_XIN: 3080}

C_ID, C_UI, C_US, C_ONE, C_IOTA, C_MAIN = 0, 128, 256, 384, 512, 640
C_LEV = C_MAIN
C_MASK = C_LEV + LEVELS * P
C_ALL = C_MASK + 2 * P
ARENA = 10304


def constants():
    i = np.arange(P)
    c = np.zeros((P, C_ALL), np.float32)
    c[:, C_ID:C_ID + P] = np.eye(P)
    c[:, C_UI:C_UI + P] = i[:, None] <= i[None, :]
    c[:, C_US:C_US + P] = i[:, None] < i[None, :]
    c[:, C_ONE:C_ONE + P] = 1.0
    c[:, C_IOTA:C_IOTA + P] = i[None, :]
    for n in range(LEVELS):
        b = 1 << n
        same = lambda w: (i[:, None] // w) == (i[None, :] // w)
        c[:, C_LEV + n * P:C_LEV + (n + 1) * P] = same(2 * b) & ~same(b)
    c[:, C_MASK:C_MASK + P] = np.where(i[None, :] > i[:, None], 0.0, NEG)
    c[:, C_MASK + P:C_MASK + 2 * P] = np.where(i[None, :] <= i[:, None], 0.0, NEG)
    return c


def band(t, k, n):
    return t[:, 0:k * n].rearrange("p (k n) -> p k n", k=k)


def build_program(nc, a, out, upto=4, dbg=None):
    with ExitStack() as ctx:
        def sb(name, shape, dt=F32):
            return ctx.enter_context(nc.sbuf_tensor(name, shape, dt))

        def sem(names):
            return [ctx.enter_context(nc.semaphore(n)) for n in names.split()]

        raw = [sb(f"raw{s}", [P, UNIT]) for s in range(NS)]
        whi = [sb(f"whi{s}", [P, UNIT], F32R) for s in range(NS)]
        wlo = [sb(f"wlo{s}", [P, UNIT], F32R) for s in range(NS)]
        xres = sb("xres", [P, TT, D])
        hThi = sb("hThi", [P, KD, T], F32R)
        hTlo = sb("hTlo", [P, KD, T], F32R)
        aThi = sb("aThi", [P, TT, FC, P], F32R)
        aTlo = sb("aTlo", [P, TT, FC, P], F32R)
        PT = sb("PT", [P, TT, P], F32R)
        cst = sb("cst", [P, C_MAIN])
        small = sb("small", [P, 480])
        flag = sb("flag", [1, 2], I32)
        arena = sb("arena", [P, ARENA])

        ident, upper, strict, ones, iota = (cst[:, c:c + P] for c in (C_ID, C_UI, C_US, C_ONE, C_IOTA))

        def view(t, at, *shape):
            v = t[:, at:at + int(np.prod(shape))]
            if len(shape) == 1:
                return v
            names = "abcd"[:len(shape)]
            return v.rearrange(f"p ({' '.join(names)}) -> p {' '.join(names)}",
                               **{k: s for k, s in zip(names[1:], shape[1:])})

        def ar(at, *shape):
            return view(arena, at, *shape)

        def sm(at, *shape):
            return view(small, at, *shape)

        def over_heads(x, n=H):
            return x.unsqueeze(1).to_broadcast([P, n, x.shape[1]])

        def along(x, n):
            return x.unsqueeze(2).to_broadcast([P, x.shape[1], n])

        xn = ar(0, TT, D)
        gain = ar(2048, D)
        Q, K, V = ar(0, H, T), ar(1024, H, T), ar(2048, H, T)
        conv_in = [ar(3072 + H * (3 + T) * n, H, 3 + T) for n in range(3)]
        l2 = ar(3072, 2, GW)
        KN = ar(3072, 2, H, P)
        Vn = ar(4096, TT, H, P)
        attnT = ar(5120, TT, H, P)
        zs = ar(6180, H, T)
        ysc = ar(7204, H, T)
        cgx = ar(8228, H, 2 + T)
        Achunk = [ar(2048, H, P), ar(2560, H, P)]
        Tm, Bm = ar(8228, H, P), ar(8740, H, P)
        Aoff, M1 = ar(9252, H, P), ar(9764, H, P)
        osq = ar(8228, 2, GW)
        S1 = ar(1024, H, P)
        wT = ar(1536, H, P)
        lev = xres[:, 0, 0:LEVELS * P].rearrange("p (n i) -> p n i", i=P)
        rowbuf = [xres[:, 1, n * GW:(n + 1) * GW].rearrange("p (h i) -> p h i", h=H) for n in range(2)]
        eG = rowbuf[1]
        qkv = ar(0, TT, D + 2 * KVH * HD)
        qT = ar(2560, KD, T)
        kdup = ar(4608, TT, KVH, 2, HD)
        kT = ar(5120, KVH, T)
        masks = ar(5632, 2, P)
        hsq = ar(5888, TT, QH + KVH, HD)
        prob = [ar(5888 + 1024 * n, 1024) for n in range(2)]
        probT = [ar(7936 + 1024 * n, 8, P) for n in range(2)]
        sil = ar(2048, TT, GW)
        actf = ar(3072, TT, GW)
        Psel = ar(4096, TT, P)
        lgt = [ar(4352 + 16 * n, TT, NE) for n in range(14)]
        slot_of = ar(4576, TT, NE + 1)
        gates = ar(4594, TT, NE + 1)
        xghi, xglo = hThi[:, :, 0:P], hTlo[:, :, 0:P]
        yhi, ylo = hThi[:, :, P:T], hTlo[:, :, P:T]

        ss, rs = sm(0, TT), sm(2, TT)
        wabhi, wablo = sb("wabhi", [P, KD * 2 * H], F32R), sb("wablo", [P, KD * 2 * H], F32R)
        wab = ar(9400, KD * 2 * H)
        beta, gdec, Gc = sm(24, TT, H), sm(32, TT, H), sm(40, TT, H)
        pre, ey, eb, t4, t5, t6 = (sm(48 + 8 * n, TT, H) for n in range(6))
        kd, kg = sm(96, H), sm(100, H)
        alog, dtb, onorm = sm(104, H), sm(108, H), sm(112, 1)
        convw, scw = sm(116, 3 * H, 4), sm(164, H, 3)
        qnw, knw, sinks = sm(176, HD), sm(240, HD), sm(304, QH)
        hss = sm(320, TT, QH + KVH)
        hrs = sm(356, TT, QH + KVH)
        smax, nmax, rsum, esink = sm(392, QH), sm(408, QH), sm(424, QH), sm(440, QH)
        rcol, gcol, cnt = sm(456, TT), sm(458, TT), sm(460, NE)

        ps = [ctx.enter_context(nc.psum_tensor(f"ps{n}", [P, GW], F32)) for n in range(8)]
        H1, H3, TP, Y = ps[0:2], ps[2:4], ps[4:6], ps[6:8]

        def heads(t):
            return t[:, :].rearrange("p (h i) -> p h i", i=P)

        def pairs(t):
            return t[:, :].rearrange("p (k t) -> p k t", k=2)

        raw_full = sem("raw_full0 raw_full1 raw_full2")
        hi_ready, lo_ready, unit_used = sem("hi_ready lo_ready unit_used")
        dve_step, act_step = sem("dve_step act_step")
        x_in, cst_in, par_in, wab_in, lev_in, gain_in, x_again, mask_in = sem(
            "x_in cst_in par_in wab_in lev_in gain_in x_again mask_in")
        n_sq, n_ms, n_rt, xn_ready, hT_ps, hThi_ready, hT_ready = sem(
            "n_sq n_ms n_rt xn_ready hT_ps hThi_ready hT_ready")
        out_ps, out_added = sem("out_ps out_added")
        sil_ready, a_ready, aT_ps, aThi_ready, aTlo_ready, y_done, y_added = sem(
            "sil_ready a_ready aT_ps aThi_ready aTlo_ready y_done y_added")
        steps = {"dve": 0, "act": 0}

        def linker(eng, name, s):
            def link(ins):
                steps[name] += 1
                ins.then_inc(s, 1)
                eng.wait_ge(s, steps[name])
            return link

        def load(sp, u, s, dst, src):
            if not (isinstance(u, int) and u < NS):
                sp.wait_ge(lo_ready, 2 * (u - NS + 1))
            sp.dma_start(dst, src).then_inc(raw_full[s], 16)

        def split_hi(act, u, s, n, size=UNIT):
            act.wait_ge(raw_full[s], 16 * (n + 1))
            if not (isinstance(u, int) and u < NS):
                act.wait_ge(unit_used, u - NS + 1)
            for h in range(2):
                part = slice(h * size // 2, (h + 1) * size // 2)
                act.copy(whi[s][:, part], raw[s][:, part]).then_inc(hi_ready, 1)

        def split_lo(dve, u, s, size=UNIT, halves=(0, 1)):
            for h in halves:
                part = slice(h * size // 2, (h + 1) * size // 2)
                dve.wait_ge(hi_ready, 2 * u + h + 1)
                dve.tensor_tensor(wlo[s][:, part], raw[s][:, part], whi[s][:, part].bitcast(F32),
                                  ALU.subtract).then_inc(lo_ready, 1)

        def hi_u(act, u, size=UNIT):
            split_hi(act, u, u % NS, u // NS, size)

        def lo_u(dve, u, size=UNIT):
            split_lo(dve, u, u % NS, size)

        def product(pe, to, lhi, llo, rhi, rlo, first, last):
            pe.matmul(to, lhi, rhi, start=first, stop=False)
            pe.matmul(to, lhi, rlo, start=False, stop=False)
            return pe.matmul(to, llo, rhi, start=False, stop=last)

        def tokens_by_columns(pe, u, to, tile, n=GW, s=None, width=P, left=None):
            s = u % NS if s is None else s
            lh, ll = left or (hThi[:, :, tile * P:tile * P + P], hTlo[:, :, tile * P:tile * P + P])
            wh, wl = band(whi[s], KD, n), band(wlo[s], KD, n)
            for k in range(KD):
                if k % 4 == 0 and tile == 0:
                    pe.wait_ge(lo_ready, 2 * u + k // 4 + 1)
                ins = product(pe, to, lh[:, k], ll[:, k], wh[:, k], wl[:, k], k == 0, k == KD - 1)
            return ins

        def act_norm(act, n, src):
            act.wait_ge(src[0], src[1])
            for t in range(TT):
                act.activation(xn[:, t, :], xres[:, t, :], ACT.Square,
                               accum_out=ss[:, t:t + 1]).then_inc(n_sq, 1)
            act.wait_ge(n_ms, n + 1)
            act.activation(rs, ss, ACT.Sqrt).then_inc(n_rt, 1)
            for b in range(4):
                act.wait_ge(hT_ps, 4 * n + b + 1)
                act.copy(hThi[:, 2 * b:2 * b + 2, :], pairs(ps[b])).then_inc(hThi_ready, 1)

        def dve_norm(dve, n, link):
            dve.wait_ge(n_sq, TT * (n + 1))
            dve.tensor_scalar(ss, ss, 1.0 / D, EPS, ALU.mult, ALU.add).then_inc(n_ms, 1)
            dve.wait_ge(n_rt, n + 1)
            link(dve.reciprocal(rs, rs))
            dve.wait_ge(gain_in, 16 * (n + 1))
            for t in range(TT):
                dve.scalar_tensor_tensor(xn[:, t, :], xres[:, t, :], rs[:, t:t + 1], gain, ALU.mult,
                                         ALU.mult).then_inc(xn_ready, 1)
            dve_transposed(dve, 4 * n)

        def dve_transposed(dve, n0):
            for b in range(4):
                dve.wait_ge(hThi_ready, n0 + b + 1)
                dve.tensor_tensor(hTlo[:, 2 * b:2 * b + 2, :], pairs(ps[b]),
                                  hThi[:, 2 * b:2 * b + 2, :].bitcast(F32), ALU.subtract).then_inc(hT_ready, 1)

        def pe_norm(pe, n):
            pe.wait_ge(xn_ready, TT * (n + 1))
            for k in range(KD):
                for t in range(TT):
                    ins = pe.transpose(pairs(ps[k // 2])[:, k % 2, t * P:t * P + P],
                                       xn[:, t, k * P:k * P + P], ident)
                if k % 2:
                    ins.then_inc(hT_ps, 1)
            pe.wait_ge(hT_ready, 4 * (n + 1))

        def even_unit(u):
            if u < U_OUT0:
                return band(raw[u % NS], KD, GW), column_block(a["ev_w_in"][0], EVEN_COL[u])
            return band(raw[u % NS], KD, GW), column_block(a["ev_w_out"][0], (u - U_OUT0) * GW)

        def column_block(w, c0, n=GW):
            return w.rearrange("(k p) n -> p k n", p=P)[:, :, c0:c0 + n]

        w1f, w3f = (a[n][0].rearrange("(k p) n -> p k n", p=P) for n in ("ev_ffn_w1", "ev_ffn_w3"))
        w2f = a["ev_ffn_w2"][0].rearrange("(b c p) n -> b p c n", p=P, c=FC)
        w1m, w3m = (a[n][0].rearrange("e (k p) n -> e p k n", p=P) for n in ("od_moe_w1", "od_moe_w3"))
        w2m = a["od_moe_w2"][0].rearrange("e (b c p) n -> (e b) p c n", p=P, c=FC)

        def ffn_col(w):
            return lambda i: w[:, :, bass.ds(i * GW, GW)]

        def moe_col(w, e):
            return lambda i: w[bass.ds(e, 1), :, :, bass.ds(i * GW, GW)].rearrange("e p k n -> p (e k) n")

        ffn_down = lambda i: w2f[bass.ds(i, 1)].rearrange("b p c n -> p (b c) n")

        def moe_down(e):
            return lambda i: w2m[bass.ds(e * NF + i, 1)].rearrange("b p c n -> p (b c) n")

        def swiglu_loads(sp, u0, w1, w3, w2):
            load(sp, u0, 0, band(raw[0], KD, GW), w1(0))
            load(sp, u0 + 1, 1, band(raw[1], KD, GW), w3(0))
            with sp.Fori(1, NF) as i:
                load(sp, u0 + 3 * i - 1, 2, band(raw[2], KD, GW), w1(i))
                load(sp, u0 + 3 * i, 0, band(raw[0], KD, GW), w3(i))
                load(sp, u0 + 3 * i + 1, 1, band(raw[1], FC, D), w2(i - 1))
            load(sp, u0 + 3 * NF - 1, 2, band(raw[2], FC, D), w2(NF - 1))

        def act_silu(act, tiles, u, g):
            act.wait_ge(unit_used, u + 1)
            if not (isinstance(g, int) and g == 0):
                act.wait_ge(a_ready, g)
            for t in range(tiles):
                act.activation(sil[:, t, :], H1[t][:, :], ACT.Silu).then_inc(sil_ready, 1)

        def act_aT(act, tiles, g):
            for t in range(tiles):
                act.wait_ge(aT_ps, g + t + 1)
                act.copy(aThi[:, t], TP[t][:, :].rearrange("p (c i) -> p c i", c=FC)).then_inc(aThi_ready, 1)

        def dve_gate(dve, tiles, u, g):
            dve.wait_ge(unit_used, u + 1)
            for t in range(tiles):
                dve.wait_ge(sil_ready, g + t + 1)
                dve.tensor_tensor(actf[:, t, :], sil[:, t, :], H3[t][:, :], ALU.mult).then_inc(a_ready, 1)

        def dve_aT(dve, tiles, g):
            for t in range(tiles):
                dve.wait_ge(aThi_ready, g + t + 1)
                dve.tensor_tensor(aTlo[:, t], TP[t][:, :].rearrange("p (c i) -> p c i", c=FC),
                                  aThi[:, t].bitcast(F32), ALU.subtract).then_inc(aTlo_ready, 1)

        def pe_up(pe, u, s, to, tiles, left=None):
            for t in range(tiles):
                ins = tokens_by_columns(pe, u, to[t][:, :], t, s=s, left=left)
            ins.then_inc(unit_used, 1)

        def pe_turn(pe, tiles, g):
            for t in range(tiles):
                pe.wait_ge(a_ready, g + t + 1)
                for c in range(FC):
                    ins = pe.transpose(TP[t][:, c * P:c * P + P], actf[:, t, c * P:c * P + P], ident)
                ins.then_inc(aT_ps, 1)

        def down(pe, to, t, s, half, first, last):
            wh, wl = band(whi[s], FC, D), band(wlo[s], FC, D)
            n = slice(half * GW, half * GW + GW)
            for c in range(FC):
                ins = product(pe, to, aThi[:, t, c], aTlo[:, t, c], wh[:, c, n], wl[:, c, n],
                              first and c == 0, last and c == FC - 1)
            return ins
        (pads, wab_hi, wab_lo, ab_done, proj_taken, gates_in, gates_exp, g_ready, gc_ps,
         conv_done, silu_done, l2_sq, l2_ps, l2_ms, l2_rt, l2_done, row_ready, row_ps, eG_ready,
         diff_ready, dec_exp, nat_ps, nat_ready, kk_ps, kk_taken, qdec_ready, tri_init, aoff_ready,
         m1_ps, m1_ready, upd_ps, T_ready, B_ready, u_ps, u_ready, s1_ps, s1_ready, ws_ps, vnew_ready,
         o_ps, o_sq, o_ssq, o_ms, o_rt, mix_ready, mix_hi, mix_lo) = sem(
            "pads wab_hi wab_lo ab_done proj_taken gates_in gates_exp g_ready gc_ps "
            "conv_done silu_done l2_sq l2_ps l2_ms l2_rt l2_done row_ready row_ps eG_ready "
            "diff_ready dec_exp nat_ps nat_ready kk_ps kk_taken qdec_ready tri_init aoff_ready "
            "m1_ps m1_ready upd_ps T_ready B_ready u_ps u_ready s1_ps s1_ready ws_ps vnew_ready "
            "o_ps o_sq o_ssq o_ms o_rt mix_ready mix_hi mix_lo")
        PROJ = [ps[4:6], ps[6:8]]
        PAIR = [slice(0, 2), slice(2, 4)]

        with nc.Block() as block:
            @block.sync
            def _(sp):
                sp.dma_start(xres[:, :, :], a["x"][0].rearrange("(t p) d -> p t d", p=P)).then_inc(x_in, 16)
                for u in range(U_FFN):
                    load(sp, u, u % NS, *even_unit(u))

            @block.scalar
            def _(act):
                act.dma_start(cst[:, :], a["consts"][:, 0:C_MAIN]).then_inc(cst_in, 16)
                act.dma_start(gain, a["ev_norm1"].to_broadcast([P, D])).then_inc(gain_in, 16)
                act.dma_start(wab.rearrange("p (k n) -> p k n", k=KD),
                              column_block(a["ev_w_in"][0], 4 * GW, 2 * H)).then_inc(wab_in, 16)
                act.dma_start(small[:, 104:320], a["params"]).then_inc(par_in, 16)
                act_norm(act, 0, (x_in, 16))
                act.wait_ge(wab_in, 16)
                act.copy(wabhi[:, :], wab).then_inc(wab_hi, 1)
                for u in (U_Q, U_K, U_V):
                    hi_u(act, u)
                act.wait_ge(xn_ready, 2)
                act.dma_start(lev, a["consts"][:, C_LEV:C_MASK].rearrange("p (n i) -> p n i", i=P)).then_inc(lev_in, 16)

                def take(n, dst):
                    act.wait_ge(unit_used, n + 1)
                    for b in range(2):
                        act.copy(dst[:, PAIR[b], :], pairs(PROJ[n % 2][b])).then_inc(proj_taken, 1)

                act.wait_ge(gates_in, 1)
                act.activation(ey, ey, ACT.Exp).then_inc(gates_exp, 1)
                act.activation(eb, eb, ACT.Exp).then_inc(gates_exp, 1)
                act.activation(alog, alog, ACT.Exp).then_inc(gates_exp, 1)
                act.wait_ge(pads, 1)
                for n in range(3):
                    take(n, conv_in[n][:, :, 3:3 + T])
                    hi_u(act, U_CG + n)
                take(3, cgx[:, :, 2:2 + T])
                hi_u(act, U_Z)
                for n, x in enumerate((Q, K, V)):
                    act.wait_ge(conv_done, n + 1)
                    act.activation(x, x, ACT.Silu).then_inc(silu_done, 1)
                act.wait_ge(unit_used, 7)
                for b in range(2):
                    act.activation(zs[:, PAIR[b], :], pairs(PROJ[0][b]), ACT.Silu).then_inc(proj_taken, 1)
                for n, x in enumerate((Q, K)):
                    act.wait_ge(silu_done, n + 1)
                    if n:
                        act.wait_ge(l2_done, 1)
                    act.activation(l2.rearrange("p a b -> p (a b)"), x.rearrange("p h t -> p (h t)"),
                                   ACT.Square).then_inc(l2_sq, 1)
                    act.wait_ge(l2_ms, n + 1)
                    act.activation(l2, l2, ACT.Sqrt).then_inc(l2_rt, 1)
                for t in range(TT):
                    act.wait_ge(diff_ready, t + 1)
                    act.activation(attnT[:, t], attnT[:, t], ACT.Exp).then_inc(dec_exp, 1)
                    if t == 0:
                        act.activation(kd, kd, ACT.Exp).then_inc(dec_exp, 1)
                        act.activation(kg, Gc[:, 1, :], ACT.Exp).then_inc(dec_exp, 1)
                act.wait_ge(row_ps, 4)
                act.activation(eG, heads(ps[1]), ACT.Exp).then_inc(eG_ready, 1)
                for u in (U_OUT0, U_OUT0 + 1):
                    hi_u(act, u)
                for t in range(TT):
                    for n in range(LEVELS):
                        for b in range(2):
                            act.wait_ge(m1_ps, 2 * (LEVELS * t + n) + b + 1)
                            act.copy(M1[:, PAIR[b]], heads(ps[b])[:, 0:2]).then_inc(m1_ready, 1)
                    if t == 0:
                        act.wait_ge(u_ps, 1)
                        act.copy(Vn[:, 0], heads(ps[6])).then_inc(u_ready, 1)
                        act.wait_ge(s1_ps, 1)
                        act.copy(S1, heads(ps[7])).then_inc(s1_ready, 1)
                act.wait_ge(u_ps, 3)
                act.copy(wT, heads(ps[7])).then_inc(u_ready, 1)
                act.copy(Vn[:, 1], heads(ps[6])).then_inc(u_ready, 1)
                for t in range(TT):
                    act.wait_ge(o_ps, t + 1)
                    act.activation(osq[:, t, :], ps[2 + t][:, :], ACT.Square).then_inc(o_sq, 1)
                act.wait_ge(o_ms, 2)
                act.activation(osq, osq, ACT.Sqrt).then_inc(o_rt, 1)
                act.wait_ge(eG_ready, 1)
                act.wait_ge(qdec_ready, 1)
                act.wait_ge(aoff_ready, 4 * LEVELS)
                act.dma_start(xres[:, :, :], a["x"][0].rearrange("(t p) d -> p t d", p=P)).then_inc(x_again, 16)
                act.wait_ge(mix_ready, 2)
                for n, x in enumerate((Q, ysc)):
                    act.copy(hThi[:, 4 * n:4 * n + 4, :], x).then_inc(mix_hi, 1)
                act.dma_start(gain, a["ev_norm2"].to_broadcast([P, D])).then_inc(gain_in, 16)

            @block.vector
            def _(dve):
                link = linker(dve, "dve", dve_step)
                for n in range(3):
                    dve.memset(conv_in[n][:, :, 0:3], 0.0)
                dve.memset(cgx[:, :, 0:2], 0.0).then_inc(pads, 1)
                dve_norm(dve, 0, link)
                dve.wait_ge(wab_hi, 1)
                dve.tensor_tensor(wablo[:, :], wab, wabhi[:, :].bitcast(F32), ALU.subtract).then_inc(wab_lo, 1)
                for u in (U_Q, U_K):
                    lo_u(dve, u)
                dve.wait_ge(ab_done, 1)
                dve.wait_ge(par_in, 16)
                ab = ps[0][:, 0:4 * H].rearrange("p (t n) -> p t n", t=TT)
                link(dve.tensor_tensor(pre, ab[:, :, 0:H], over_heads(dtb, TT), ALU.add))
                link(dve.tensor_scalar(t4, pre, -1.0, None, ALU.mult))
                link(dve.tensor_tensor(ey, pre, t4, ALU.min))
                dve.tensor_scalar(eb, ab[:, :, H:2 * H], -1.0, None, ALU.mult).then_inc(gates_in, 1)
                lo_u(dve, U_V)
                dve.wait_ge(gates_exp, 3)
                link(dve.tensor_scalar(t4, ey, 2.0, None, ALU.add))
                link(dve.reciprocal(t4, t4))
                link(dve.tensor_tensor(t4, t4, ey, ALU.mult))
                link(dve.tensor_tensor(t5, t4, t4, ALU.mult))
                link(dve.tensor_scalar(t6, t5, 1.0 / 19, None, ALU.mult))
                for n in range(8, 0, -1):
                    link(dve.scalar_tensor_tensor(t6, t6, 1.0 / (2 * n + 1), t5, ALU.add, ALU.mult))
                link(dve.scalar_tensor_tensor(t6, t6, 1.0, t4, ALU.add, ALU.mult))
                link(dve.tensor_scalar(pre, pre, 0.0, None, ALU.max))
                link(dve.scalar_tensor_tensor(t6, t6, 2.0, pre, ALU.mult, ALU.add))
                link(dve.scalar_tensor_tensor(gdec, t6, -1.0, over_heads(alog, TT), ALU.mult, ALU.mult))
                link(dve.tensor_scalar(eb, eb, 1.0, None, ALU.add))
                dve.reciprocal(beta, eb).then_inc(g_ready, 1)
                dve.wait_ge(gc_ps, 1)
                dve.wait_ge(g_ready, 1)
                link(dve.tensor_copy(Gc, ps[0][:, 32:32 + 2 * H].rearrange("p (t n) -> p t n", t=TT)))
                lo_u(dve, U_CG)

                def conv(dst, src, w, taps):
                    for c in range(H):
                        dve.tensor_scalar(dst[:, c, :], src[:, c, 0:T], w[:, c, 0:1], None, ALU.mult).then_inc(dve_step, 1)
                    steps["dve"] += H
                    dve.wait_ge(dve_step, steps["dve"])
                    for j in range(1, taps):
                        for c in range(H):
                            ins = dve.scalar_tensor_tensor(dst[:, c, :], src[:, c, j:j + T], w[:, c, j:j + 1],
                                                           dst[:, c, :], ALU.mult, ALU.add)
                            if j < taps - 1:
                                ins.then_inc(dve_step, 1)
                        if j < taps - 1:
                            steps["dve"] += H
                            dve.wait_ge(dve_step, steps["dve"])
                    return ins

                for n, x in enumerate((Q, K, V)):
                    dve.wait_ge(proj_taken, 2 * n + 2)
                    conv(x, conv_in[n], convw[:, H * n:H * n + H], 4).then_inc(conv_done, 1)
                    if n < 2:
                        lo_u(dve, U_XIN + n)
                dve.wait_ge(proj_taken, 8)
                dve.wait_ge(unit_used, 5)
                for b in range(2):
                    x = cgx[:, PAIR[b], 2:2 + T]
                    dve.tensor_tensor(x, x, pairs(PROJ[0][b]), ALU.mult).then_inc(proj_taken, 1)
                lo_u(dve, U_Z)
                dve.wait_ge(proj_taken, 10)
                link(conv(ysc, cgx, scw, 3))
                dve.wait_ge(unit_used, 6)
                for b in range(2):
                    x = ysc[:, PAIR[b], :]
                    dve.tensor_tensor(x, x, pairs(PROJ[1][b]), ALU.mult).then_inc(proj_taken, 1)
                for n, x in enumerate((Q, K)):
                    dve.wait_ge(l2_ps, 2 * n + 2)
                    for b in range(2):
                        ins = dve.tensor_scalar(l2[:, b, :], ps[2 * n + b][:, :], EPS, None, ALU.add)
                    ins.then_inc(l2_ms, 1)
                    dve.wait_ge(l2_rt, n + 1)
                    link(dve.reciprocal(l2, l2))
                    dve.scalar_tensor_tensor(x.rearrange("p h t -> p (h t)"), x.rearrange("p h t -> p (h t)"),
                                             float(P) ** -0.5 if n == 0 else 1.0,
                                             l2.rearrange("p a b -> p (a b)"), ALU.mult, ALU.mult).then_inc(l2_done, 1)
                for n in range(4):
                    src, tri = ((gdec, upper), (beta, ident))[n // 2]
                    if n >= 2:
                        dve.wait_ge(row_ps, n - 1)
                    dve.tensor_tensor(rowbuf[n % 2], over_heads(tri), along(src[:, n % 2, :], P),
                                      ALU.mult).then_inc(row_ready, 1)
                for t in range(TT):
                    dve.wait_ge(row_ps, t + 1)
                    link(dve.tensor_tensor(attnT[:, t], heads(ps[t]), along(Gc[:, t, :], P), ALU.subtract))
                    if t == 0:
                        link(dve.tensor_tensor(kd, heads(ps[0])[:, :, P - 1], Gc[:, 0, :], ALU.subtract))
                    dve.tensor_scalar(attnT[:, t], attnT[:, t], 0.0, None, ALU.min).then_inc(diff_ready, 1)
                dve.wait_ge(dec_exp, 3)
                link(dve.tensor_tensor(kg, kg, beta[:, 1, :], ALU.mult))
                for n, (dst, scale) in enumerate(((KN[:, 0], kd), (KN[:, 1], kg), (Vn[:, 0], beta[:, 0, :]),
                                                  (Vn[:, 1], beta[:, 1, :]))):
                    dve.wait_ge(nat_ps, n + 1)
                    dve.tensor_tensor(dst, heads(ps[4 + n]), along(scale, P), ALU.mult).then_inc(nat_ready, 1)
                dve.wait_ge(row_ps, 4)
                for t in range(TT):
                    dve.wait_ge(dec_exp, 1 if t == 0 else 4)
                    link(dve.tensor_tensor(attnT[:, t], attnT[:, t], over_heads(upper), ALU.mult))
                    dve.wait_ge(kk_ps, 2 * t + 2)
                    link(dve.tensor_tensor(Achunk[t], heads(ps[4 + 2 * t]), attnT[:, t], ALU.mult))
                    link(dve.tensor_tensor(Achunk[t], heads(ps[2 + t]), Achunk[t], ALU.mult))
                    link(dve.tensor_tensor(Achunk[t], Achunk[t], over_heads(strict), ALU.mult))
                    dve.tensor_tensor(attnT[:, t], heads(ps[5 + 2 * t]), attnT[:, t], ALU.mult).then_inc(kk_taken, 1)
                dve.wait_ge(eG_ready, 1)
                dve.tensor_tensor(Q[:, :, P:T], Q[:, :, P:T], eG, ALU.mult).then_inc(qdec_ready, 1)
                for u in (U_OUT0, U_OUT0 + 1):
                    lo_u(dve, u)
                dve.wait_ge(lev_in, 16)
                for t in range(TT):
                    if t:
                        dve.wait_ge(u_ps, 1)
                    dve.tensor_copy(Tm, over_heads(ident)).then_inc(T_ready, 2)
                    dve.tensor_copy(Bm, over_heads(ident)).then_inc(B_ready, 2)
                    for n in range(LEVELS):
                        j = LEVELS * t + n
                        for b in range(2):
                            if j:
                                dve.wait_ge(m1_ps, 2 * (j - 1) + b + 1)
                            dve.tensor_tensor(Aoff[:, PAIR[b]], Achunk[t][:, PAIR[b]], over_heads(lev[:, n], 2),
                                              ALU.mult).then_inc(aoff_ready, 1)
                        for b in range(2):
                            dve.wait_ge(upd_ps, 2 * j + b + 1)
                            dve.wait_ge(T_ready, 2 * (j + t) + b + 1 if n else 2 * (j + t) + 2)
                            dve.tensor_tensor(Tm[:, PAIR[b]], Tm[:, PAIR[b]], heads(ps[2 + b])[:, 0:2],
                                              ALU.subtract).then_inc(T_ready, 1)
                            dve.wait_ge(B_ready, 2 * (j + t) + b + 1 if n else 2 * (j + t) + 2)
                            dve.tensor_tensor(Bm[:, PAIR[b]], Bm[:, PAIR[b]], heads(ps[4 + b])[:, 0:2],
                                              ALU.subtract).then_inc(B_ready, 1)
                dve.wait_ge(ws_ps, 1)
                dve.wait_ge(u_ready, 3)
                dve.tensor_tensor(Vn[:, 1], Vn[:, 1], heads(ps[0]), ALU.subtract).then_inc(vnew_ready, 1)
                for t in range(TT):
                    dve.wait_ge(o_ssq, t + 1)
                    dve.tensor_scalar(osq[:, t, :], ps[4 + t][:, :], 1.0 / P, EPS, ALU.mult, ALU.add).then_inc(o_ms, 1)
                dve.wait_ge(o_rt, 1)
                link(dve.reciprocal(osq, osq))
                for t in range(TT):
                    link(dve.tensor_tensor(osq[:, t, :], osq[:, t, :], ps[2 + t][:, :], ALU.mult))
                    dve.scalar_tensor_tensor(Q[:, :, t * P:t * P + P], osq[:, t, :].rearrange("p (h i) -> p h i", h=H),
                                             onorm, zs[:, :, t * P:t * P + P], ALU.mult, ALU.mult).then_inc(mix_ready, 1)
                for n, x in enumerate((Q, ysc)):
                    dve.wait_ge(mix_hi, n + 1)
                    dve.tensor_tensor(hTlo[:, 4 * n:4 * n + 4, :], x, hThi[:, 4 * n:4 * n + 4, :].bitcast(F32),
                                      ALU.subtract).then_inc(mix_lo, 1)
                dve.wait_ge(x_again, 16)
                for n in range(4):
                    h, t = divmod(n, 2)
                    dve.wait_ge((out_ps, unit_used)[t], (h + 1, U_OUT0 + h + 1)[t])
                    x = xres[:, t, h * GW:h * GW + GW]
                    dve.tensor_tensor(x, x, ps[n][:, :], ALU.add).then_inc(out_added, 1)

            @block.tensor
            def _(pe):
                pe.wait_ge(cst_in, 16)
                pe_norm(pe, 0)
                pe.wait_ge(wab_lo, 1)
                wh, wl = band(wabhi, KD, 2 * H), band(wablo, KD, 2 * H)
                for t in range(TT):
                    tok = slice(t * P, t * P + P)
                    for k in range(KD):
                        ins = product(pe, ps[0][:, t * 2 * H:(t + 1) * 2 * H], hThi[:, k, tok], hTlo[:, k, tok],
                                      wh[:, k], wl[:, k], k == 0, k == KD - 1)
                ins.then_inc(ab_done, 1)

                def project(n):
                    u = n
                    if n >= 2:
                        pe.wait_ge(proj_taken, 2 * (n - 1))
                    wh, wl = band(whi[u % NS], KD, GW), band(wlo[u % NS], KD, GW)
                    pe.wait_ge(lo_ready, 2 * u + 2)
                    for c in range(H):
                        ch = slice(c * P, c * P + P)
                        to = pairs(PROJ[n % 2][c // 2])[:, c % 2, :]
                        for k in range(KD):
                            ins = product(pe, to, wh[:, k, ch], wl[:, k, ch], hThi[:, k, :], hTlo[:, k, :],
                                          k == 0, k == KD - 1)
                    ins.then_inc(unit_used, 1)

                project(0)
                project(1)
                pe.wait_ge(g_ready, 1)
                for t in range(TT):
                    ins = pe.matmul(ps[0][:, 32 + t * H:32 + t * H + H], upper, gdec[:, t, :], start=True, stop=True)
                ins.then_inc(gc_ps, 1)
                for n in range(2, 7):
                    project(n)
                for n in range(2):
                    pe.wait_ge(l2_sq, n + 1)
                    for b in range(2):
                        pe.matmul(ps[2 * n + b][:, :], ones, l2[:, b, :], start=True, stop=True).then_inc(l2_ps, 1)
                pe.wait_ge(l2_done, 2)
                for n in range(4):
                    pe.wait_ge(row_ready, n + 1)
                    pe.matmul(ps[n][:, :], ones, rowbuf[n % 2].rearrange("p h i -> p (h i)"), start=True,
                              stop=True).then_inc(row_ps, 1)
                pe.wait_ge(proj_taken, 14)
                pe.wait_ge(silu_done, 3)
                for n in range(4):
                    t = n % 2
                    for h in range(H):
                        ins = pe.transpose(heads(ps[4 + n])[:, h, :], (K, V)[n // 2][:, h, t * P:t * P + P], ident)
                    ins.then_inc(nat_ps, 1)
                pe.wait_ge(nat_ready, 4)
                for n in range(4):
                    t = n // 2
                    tok = slice(t * P, t * P + P)
                    for h in range(H):
                        ins = pe.matmul(heads(ps[4 + n])[:, h, :], K[:, h, tok], (K, Q)[n % 2][:, h, tok],
                                        start=True, stop=True)
                    ins.then_inc(kk_ps, 1)
                pe.wait_ge(kk_taken, 2)
                pe.wait_ge(eG_ready, 1)
                for t in range(TT):
                    for n in range(LEVELS):
                        j = LEVELS * t + n
                        for b in range(2):
                            pe.wait_ge(aoff_ready, 2 * j + b + 1)
                            pe.wait_ge(T_ready, 2 * (j + t) + 2 + (b if n else 0) - (1 if n else 0))
                            for h in range(2):
                                ins = pe.matmul(heads(ps[b])[:, h, :], Aoff[:, 2 * b + h], Tm[:, 2 * b + h],
                                                start=True, stop=True)
                            ins.then_inc(m1_ps, 1)
                        for b in range(2):
                            pe.wait_ge(m1_ready, 2 * j + b + 1)
                            pe.wait_ge(B_ready, 2 * (j + t) + 2 + (b if n else 0) - (1 if n else 0))
                            for h in range(2):
                                pe.matmul(heads(ps[2 + b])[:, h, :], Bm[:, 2 * b + h], M1[:, 2 * b + h],
                                          start=True, stop=True)
                            for h in range(2):
                                ins = pe.matmul(heads(ps[4 + b])[:, h, :], M1[:, 2 * b + h], Bm[:, 2 * b + h],
                                                start=True, stop=True)
                            ins.then_inc(upd_ps, 1)
                    pe.wait_ge(B_ready, 2 * (LEVELS + 1) * (t + 1))
                    if t:
                        pe.wait_ge(s1_ready, 1)
                    for h in range(H):
                        ins = pe.matmul(heads(ps[6])[:, h, :], Bm[:, h], Vn[:, t, h], start=True, stop=True)
                    ins.then_inc(u_ps, 1)
                    if t == 0:
                        pe.wait_ge(u_ready, 1)
                        for h in range(H):
                            ins = pe.matmul(heads(ps[7])[:, h, :], KN[:, 0, h], Vn[:, 0, h], start=True, stop=True)
                        ins.then_inc(s1_ps, 1)
                for h in range(H):
                    ins = pe.matmul(heads(ps[7])[:, h, :], KN[:, 1, h], Bm[:, h], start=True, stop=True)
                ins.then_inc(u_ps, 1)
                for h in range(H):
                    ins = pe.matmul(heads(ps[2])[:, h, :], Vn[:, 0, h], attnT[:, 0, h], start=True, stop=True)
                ins.then_inc(o_ps, 1)
                pe.wait_ge(u_ready, 2)
                for h in range(H):
                    ins = pe.matmul(heads(ps[0])[:, h, :], wT[:, h], S1[:, h], start=True, stop=True)
                ins.then_inc(ws_ps, 1)
                pe.wait_ge(vnew_ready, 1)
                pe.wait_ge(qdec_ready, 1)
                for h in range(H):
                    pe.matmul(heads(ps[3])[:, h, :], S1[:, h], Q[:, h, P:T], start=True, stop=False)
                    ins = pe.matmul(heads(ps[3])[:, h, :], Vn[:, 1, h], attnT[:, 1, h], start=False, stop=True)
                ins.then_inc(o_ps, 1)
                for t in range(TT):
                    pe.wait_ge(o_sq, t + 1)
                    pe.matmul(ps[4 + t][:, :], ones, osq[:, t, :], start=True, stop=True).then_inc(o_ssq, 1)
                pe.wait_ge(mix_lo, 2)
                for h in range(2):
                    u = U_OUT0 + h
                    for t in range(TT):
                        ins = tokens_by_columns(pe, u, ps[2 * h + t][:, :], t)
                        ins.then_inc((out_ps, unit_used)[t], 1)
        if upto >= 2:
          with nc.Block() as block:
            u0, n0 = U_FFN, U_FFN // NS

            def unit_of(i):
                return u0 + 3 * i - 1, u0 + 3 * i, u0 + 3 * i + 1

            def down_unit(i):
                return u0 + 3 * NF - 1 if isinstance(i, int) and i == NF - 1 else u0 + 3 * i + 4

            @block.sync
            def _(sp):
                swiglu_loads(sp, u0, ffn_col(w1f), ffn_col(w3f), ffn_down)

            @block.scalar
            def _(act):
                act_norm(act, 1, (out_added, 4))
                split_hi(act, u0, 0, n0)
                split_hi(act, u0 + 1, 1, n0)
                act_silu(act, TT, u0, 0)
                with act.Fori(1, NF) as i:
                    w1, w3, w2 = unit_of(i)
                    split_hi(act, w1, 2, n0 + i - 1)
                    split_hi(act, w3, 0, n0 + i)
                    act_aT(act, TT, 2 * i - 2)
                    split_hi(act, w2, 1, n0 + i)
                    act_silu(act, TT, w1, 2 * i)
                act_aT(act, TT, 2 * NF - 2)
                split_hi(act, u0 + 3 * NF - 1, 2, n0 + NF - 1)
                act.wait_ge(xn_ready, 4)
                act.dma_start(gain, a["od_norm1"].to_broadcast([P, D])).then_inc(gain_in, 16)

            @block.vector
            def _(dve):
                link = linker(dve, "dve", dve_step)
                dve_norm(dve, 1, link)

                def add_y(i, part):
                    for n in part:
                        t, h = divmod(n, 2)
                        if n < 3:
                            dve.wait_ge(y_done, 3 * i + n + 1)
                        else:
                            dve.wait_ge(unit_used, down_unit(i) + 1)
                        if not (isinstance(i, int) and i == 0):
                            dve.wait_ge(y_added, 4 * i + n - 3)
                        x = xres[:, t, h * GW:h * GW + GW]
                        dve.tensor_tensor(x, x, Y[h][:, :], ALU.add).then_inc(y_added, 1)

                split_lo(dve, u0, 0)
                split_lo(dve, u0 + 1, 1)
                dve_gate(dve, TT, u0 + 1, 0)
                split_lo(dve, u0 + 2, 2)

                def step(i, last):
                    w1, w3, w2 = unit_of(i)
                    split_lo(dve, w3, 0)
                    dve_aT(dve, TT, 2 * i - 2)
                    split_lo(dve, w2, 1)
                    dve_gate(dve, TT, w3, 2 * i)
                    if not last:
                        split_lo(dve, w1 + 3, 2)
                    add_y(i - 1, range(4))

                step(1, False)
                with dve.Fori(2, NF - 1) as i:
                    step(i, False)
                step(NF - 1, True)
                dve_aT(dve, TT, 2 * NF - 2)
                split_lo(dve, u0 + 3 * NF - 1, 2)
                add_y(NF - 1, range(4))

            @block.tensor
            def _(pe):
                pe_norm(pe, 1)

                def turn_down(i, s, free):
                    pe.wait_ge(aTlo_ready, 2 * i + 2)
                    for n in range(4):
                        t, h = divmod(n, 2)
                        if free or n >= 2:
                            pe.wait_ge(y_added, 4 * i + n - 1)
                        if n == 0:
                            pe.wait_ge(lo_ready, 2 * down_unit(i) + 2)
                        down(pe, Y[h][:, :], t, s, h, True, True).then_inc(y_done if n < 3 else unit_used, 1)

                pe_up(pe, u0, 0, H1, TT)
                pe_up(pe, u0 + 1, 1, H3, TT)
                pe_turn(pe, TT, 0)

                def step(i):
                    w1, w3, w2 = unit_of(i)
                    pe.wait_ge(sil_ready, 2 * i)
                    pe_up(pe, w1, 2, H1, TT)
                    pe_up(pe, w3, 0, H3, TT)
                    turn_down(i - 1, 1, not (isinstance(i, int) and i == 1))
                    pe_turn(pe, TT, 2 * i)

                step(1)
                with pe.Fori(2, NF) as i:
                    step(i)
                turn_down(NF - 1, 2, True)
        (qkv_ps, qkv_taken, h_sq, h_ms, h_rt, qk_ready, qT_ps, qT_ready, kT_ready, sc_ps, neg_max,
         p_ready, pT_ps, pT_ready, av_ps, es_in, es_exp, ao_ready, aoT_ps, aoT_hi, aoT_lo) = sem(
            "qkv_ps qkv_taken h_sq h_ms h_rt qk_ready qT_ps qT_ready kT_ready sc_ps neg_max "
            "p_ready pT_ps pT_ready av_ps es_in es_exp ao_ready aoT_ps aoT_hi aoT_lo")
        if upto >= 3:
          QK = QH + KVH

          def place(h):
              return 2 * (h % 2) + h // 2

          with nc.Block() as block:
            @block.sync
            def _(sp):
                for h in range(2):
                    load(sp, U_IN1 + h, (U_IN1 + h) % NS, band(raw[(U_IN1 + h) % NS], KD, GW),
                         column_block(a["od_w_in"][0], h * GW))
                u = U_IN1 + 2
                load(sp, u, u % NS, band(raw[u % NS], KD, GW // 2), column_block(a["od_w_in"][0], 2 * GW, GW // 2))
                for h in range(2):
                    u = U_OUT1 + h
                    load(sp, u, u % NS, band(raw[u % NS], KD, GW), column_block(a["od_w_out"][0], h * GW))
                u = U_ROUTER
                load(sp, u, u % NS, band(raw[u % NS], KD, NE), column_block(a["od_router"][0], 0, NE))

            @block.scalar
            def _(act):
                act.dma_start(masks, a["consts"][:, C_MASK:C_ALL].rearrange("p (a i) -> p a i", a=2)).then_inc(mask_in, 16)
                act_norm(act, 2, (y_added, 4 * NF))
                hi_u(act, U_IN1)
                hi_u(act, U_IN1 + 1)
                hi_u(act, U_IN1 + 2, UNIT // 2)
                for c in range(3):
                    n = GW if c < 2 else GW // 2
                    for t in range(TT):
                        if t == 0:
                            act.wait_ge(qkv_ps, c + 1)
                        else:
                            act.wait_ge(unit_used, U_IN1 + c + 1)
                        act.copy(qkv[:, t, c * GW:c * GW + n], ps[2 * c + t][:, 0:n]).then_inc(qkv_taken, 1)
                act.wait_ge(qkv_taken, 6)
                for t in range(TT):
                    act.activation(hsq[:, t], qkv[:, t, 0:QK * HD].rearrange("p (h d) -> p h d", d=HD),
                                   ACT.Square).then_inc(h_sq, 1)
                act.wait_ge(h_ms, 1)
                act.activation(hrs, hss, ACT.Sqrt).then_inc(h_rt, 1)
                hi_u(act, U_OUT1)
                hi_u(act, U_OUT1 + 1)
                for b in range(4):
                    act.wait_ge(qT_ps, b + 1)
                    act.copy(qT[:, 2 * b:2 * b + 2, :], pairs(ps[b])).then_inc(qT_ready, 1)
                for j in range(8):
                    t, g = divmod(j, 4)
                    keys = P * (1 + t)
                    act.wait_ge(neg_max, j + 1)
                    for h in range(4):
                        hh = 4 * g + h
                        at = place(h) * keys
                        x = prob[j % 2][:, at:at + keys]
                        act.activation(x, x, ACT.Exp, bias=nmax[:, hh:hh + 1],
                                       accum_out=rsum[:, hh:hh + 1]).then_inc(p_ready, 1)
                    if g == 3:
                        act.wait_ge(es_in, t + 1)
                        act.activation(esink, esink, ACT.Exp).then_inc(es_exp, 1)
                for b in range(4):
                    act.wait_ge(aoT_ps, b + 1)
                    act.copy(hThi[:, 2 * b:2 * b + 2, :], pairs(ps[b])).then_inc(aoT_hi, 1)
                act.dma_start(gain, a["od_norm2"].to_broadcast([P, D])).then_inc(gain_in, 16)

            @block.vector
            def _(dve):
                link = linker(dve, "dve", dve_step)
                dve_norm(dve, 2, link)
                lo_u(dve, U_IN1)
                lo_u(dve, U_IN1 + 1)
                lo_u(dve, U_IN1 + 2, UNIT // 2)
                for t in range(TT):
                    dve.wait_ge(h_sq, t + 1)
                    dve.tensor_reduce(hss[:, t, :], hsq[:, t], AX.X, ALU.add).then_inc(dve_step, 1)
                steps["dve"] += TT
                dve.wait_ge(dve_step, steps["dve"])
                dve.tensor_scalar(hss, hss, 1.0 / HD, EPS, ALU.mult, ALU.add).then_inc(h_ms, 1)
                dve.wait_ge(h_rt, 1)
                link(dve.reciprocal(hrs, hrs))
                for t in range(TT):
                    x = qkv[:, t, 0:QK * HD].rearrange("p (h d) -> p h d", d=HD)
                    link(dve.tensor_tensor(x, x, along(hrs[:, t, :], HD), ALU.mult))
                    dve.tensor_tensor(x[:, 0:QH], x[:, 0:QH], over_heads(qnw, QH), ALU.mult).then_inc(qk_ready, 1)
                    k = x[:, QH:QK]
                    for n in range(2):
                        dve.tensor_tensor(kdup[:, t, :, n, :], k, over_heads(knw, KVH), ALU.mult).then_inc(qk_ready, 1)
                lo_u(dve, U_OUT1)
                lo_u(dve, U_OUT1 + 1)
                dve.wait_ge(qT_ps, 5)
                dve.tensor_copy(kT, pairs(ps[4])).then_inc(kT_ready, 1)
                dve.wait_ge(mask_in, 16)

                def masked(j):
                    t, g = divmod(j, 4)
                    keys = P * (1 + t)
                    if j >= 2:
                        dve.wait_ge(pT_ps, j - 1)
                    dve.wait_ge(sc_ps, j + 1)
                    x = prob[j % 2][:, 0:4 * keys].rearrange("p (h k) -> p h k", h=4)
                    m = masks.rearrange("p a i -> p (a i)")[:, P - P * t:2 * P]
                    for b in range(2):
                        s = ps[2 * (j % 2) + b][:, 0:2 * keys].rearrange("p (h k) -> p h k", h=2)
                        link(dve.scalar_tensor_tensor(x[:, 2 * b:2 * b + 2], s, HD ** -0.5, over_heads(m, 2),
                                                      ALU.mult, ALU.add))
                    hs = slice(4 * g, 4 * g + 4)
                    if g == 0 and t:
                        dve.wait_ge(ao_ready, 2)
                    link(dve.tensor_reduce(smax[:, hs].rearrange("p (m b) -> p b m", b=2),
                                           x.rearrange("p (b m) k -> p b m k", b=2), AX.X, ALU.max))
                    link(dve.tensor_tensor(smax[:, hs], smax[:, hs], sinks[:, hs], ALU.max))
                    dve.tensor_scalar(nmax[:, hs], smax[:, hs], -1.0, None, ALU.mult).then_inc(neg_max, 1)

                def turned(j):
                    t, g = divmod(j, 4)
                    dve.wait_ge(pT_ps, j + 1)
                    if j >= 2:
                        dve.wait_ge(av_ps, j - 1)
                    for b in range(1 + t):
                        ins = dve.tensor_copy(probT[j % 2][:, 4 * b:4 * b + 4, :],
                                              ps[4 + b][:, :].rearrange("p (c i) -> p c i", c=4))
                    ins.then_inc(pT_ready, 1)

                def outputs(t):
                    dve.wait_ge(p_ready, 16 * (t + 1))
                    dve.wait_ge(es_exp, t + 1)
                    link(dve.tensor_tensor(rsum, rsum, esink, ALU.add))
                    link(dve.reciprocal(rsum, rsum))
                    dve.wait_ge(av_ps, 4 * t + 4)
                    for b in range(2):
                        dve.tensor_tensor(ao(t, b), ps[6 + b][:, :].rearrange("p (h d) -> p h d", d=HD),
                                          along(rsum[:, 8 * b:8 * b + 8], HD), ALU.mult).then_inc(ao_ready, 1)

                def ao(t, b):
                    return qkv[:, t, b * GW:b * GW + GW].rearrange("p (h d) -> p h d", d=HD)

                for t in range(TT):
                    for g in range(4):
                        masked(4 * t + g)
                        if g == 3:
                            dve.tensor_tensor(esink, sinks, smax, ALU.subtract).then_inc(es_in, 1)
                        if g:
                            turned(4 * t + g - 1)
                    turned(4 * t + 3)
                    outputs(t)
                for b in range(4):
                    dve.wait_ge(aoT_hi, b + 1)
                    dve.tensor_tensor(hTlo[:, 2 * b:2 * b + 2, :], pairs(ps[b]),
                                      hThi[:, 2 * b:2 * b + 2, :].bitcast(F32), ALU.subtract).then_inc(aoT_lo, 1)
                for n in range(4):
                    h, t = divmod(n, 2)
                    dve.wait_ge((out_ps, unit_used)[t], (3 + h, U_OUT1 + h + 1)[t])
                    x = xres[:, t, h * GW:h * GW + GW]
                    dve.tensor_tensor(x, x, ps[4 + n][:, :], ALU.add).then_inc(out_added, 1)

            @block.tensor
            def _(pe):
                pe_norm(pe, 2)
                for c in range(3):
                    n = GW if c < 2 else GW // 2
                    for t in range(TT):
                        ins = tokens_by_columns(pe, U_IN1 + c, ps[2 * c + t][:, 0:n], t, n=n)
                        ins.then_inc((qkv_ps, unit_used)[t], 1)
                pe.wait_ge(qkv_taken, 6)
                pe.wait_ge(qk_ready, 6)
                for k in range(KD):
                    for t in range(TT):
                        ins = pe.transpose(pairs(ps[k // 2])[:, k % 2, t * P:t * P + P], qkv[:, t, k * P:k * P + P], ident)
                    if k % 2:
                        ins.then_inc(qT_ps, 1)
                for g in range(KVH):
                    for t in range(TT):
                        ins = pe.transpose(pairs(ps[4])[:, g, t * P:t * P + P],
                                           kdup[:, t, g].rearrange("p n d -> p (n d)"), ident)
                ins.then_inc(qT_ps, 1)
                pe.wait_ge(qT_ready, 4)
                pe.wait_ge(kT_ready, 1)

                def scores(j):
                    t, g = divmod(j, 4)
                    if j >= 2:
                        pe.wait_ge(neg_max, j - 1)
                    for h in range(4):
                        hh = 4 * g + h
                        rows = slice(HD * (hh % 2), HD * (hh % 2) + HD)
                        keys = P * (1 + t)
                        at = (h // 2) * keys
                        ins = pe.matmul(ps[2 * (j % 2) + h % 2][:, at:at + keys], qT[rows, hh // 2, t * P:t * P + P],
                                        kT[rows, hh // GRP, 0:keys], start=True, stop=True)
                    ins.then_inc(sc_ps, 1)

                def turn(j):
                    t, g = divmod(j, 4)
                    pe.wait_ge(p_ready, 4 * j + 4)
                    if j:
                        pe.wait_ge(pT_ready, j)
                    for c in range(4 * (1 + t)):
                        ins = pe.transpose(ps[4 + c // 4][:, (c % 4) * P:(c % 4) * P + P],
                                           prob[j % 2][:, c * P:c * P + P], ident)
                    ins.then_inc(pT_ps, 1)

                def values(j):
                    t, g = divmod(j, 4)
                    pe.wait_ge(pT_ready, j + 1)
                    if t and g == 0:
                        pe.wait_ge(ao_ready, 2)
                    for h in range(4):
                        hh = 4 * g + h
                        to = ps[6 + hh // 8][:, (hh % 8) * HD:(hh % 8) * HD + HD]
                        for kb in range(1 + t):
                            v = qkv[:, kb, (QK + hh // GRP) * HD:(QK + hh // GRP + 1) * HD]
                            ins = pe.matmul(to, probT[j % 2][:, place(h) * (1 + t) + kb, :], v, start=kb == 0, stop=kb == t)
                    ins.then_inc(av_ps, 1)

                scores(0)
                for j in range(8):
                    if j + 1 < 8:
                        scores(j + 1)
                    turn(j)
                    values(j)
                pe.wait_ge(ao_ready, 4)
                for k in range(KD):
                    for t in range(TT):
                        ins = pe.transpose(pairs(ps[k // 2])[:, k % 2, t * P:t * P + P], qkv[:, t, k * P:k * P + P], ident)
                    if k % 2:
                        ins.then_inc(aoT_ps, 1)
                pe.wait_ge(aoT_lo, 4)
                for h in range(2):
                    for t in range(TT):
                        ins = tokens_by_columns(pe, U_OUT1 + h, ps[4 + 2 * h + t][:, :], t)
                        ins.then_inc((out_ps, unit_used)[t], 1)
        (lg_done, rt_in, rt_exp, rank_in, rank_ps, slots_ready, flag_ready, sel_ready, xg_ps, xghi_ready,
         xglo_ready, PT_ps, PT_ready, yhi_ready, ylo_ready, sc_done, sc_added, out_sent, rcol_ready,
         gcol_ready) = sem(
            "lg_done rt_in rt_exp rank_in rank_ps slots_ready flag_ready sel_ready xg_ps xghi_ready "
            "xglo_ready PT_ps PT_ready yhi_ready ylo_ready sc_done sc_added out_sent rcol_ready gcol_ready")
        if upto < 4:
          with nc.Block() as block:
            @block.sync
            def _(sp):
                sp.wait_ge(gain_in, 16 * (upto + 1) if upto != 2 else 48)
                sp.wait_ge((out_added, y_added, out_added)[upto - 1], (4, 4 * NF, 8)[upto - 1])
                sp.dma_start(out[0].rearrange("(t p) d -> p t d", p=P), xres[:, :, :]).then_inc(out_sent, 16)
                sp.wait_ge(out_sent, 16)
        if upto >= 4:
          GATHER = [H1[1], H3[1]]
          SCATTER = [H1[1], H3[1], Y[0], Y[1]]
          G0 = 2 * NF

          def slots_of(t):
              return Psel[:, t, :]

          with nc.Block() as block:
            out_t = out[0].rearrange("(t p) d -> p t d", p=P)

            def units(q, e, i):
                u0 = U_MOE + U_PASS * q + 3 * NF * e
                return u0 + 3 * i - 1, u0 + 3 * i, u0 + 3 * i + 1

            def uses(q, e):
                return (U_MOE + U_PASS * q) // NS + NF * e

            def tiles(q, e, i):
                return G0 + NF * NE * q + NF * e + i

            @block.sync
            def _(sp):
                def moe_loads(q):
                    with sp.Fori(0, NE) as e:
                        swiglu_loads(sp, U_MOE + U_PASS * q + 3 * NF * e, moe_col(w1m, e), moe_col(w3m, e), moe_down(e))

                moe_loads(0)
                sp.wait_ge(sc_added, 4 * NE)
                sp.dma_start(out_t, xres[:, :, :]).then_inc(out_sent, 16)
                sp.wait_ge(out_sent, 16)
                sp.wait_ge(flag_ready, 1)
                more = sp.value_load(flag[0:1, 0:1], min_val=0, max_val=1)
                with sp.If(more == 1):
                    moe_loads(1)
                    sp.wait_ge(sc_added, 8 * NE)
                    sp.dma_start(out_t, xres[:, :, :]).then_inc(out_sent, 16)
                    sp.wait_ge(out_sent, 32)
                sp.nop()

            @block.scalar
            def _(act):
                act_norm(act, 3, (out_added, 8))
                hi_u(act, U_ROUTER, KD * NE)
                act.wait_ge(rt_in, 1)
                act.activation(lgt[13], lgt[13], ACT.Exp).then_inc(rt_exp, 1)

                def gathered(n):
                    act.wait_ge(xg_ps, n + 1)
                    for b in range(2):
                        act.copy(xghi[:, 4 * b:4 * b + 4, :], heads(GATHER[b])).then_inc(xghi_ready, 1)

                def opening_silu(q, e):
                    act_silu(act, 1, U_MOE + U_PASS * q + 3 * NF * e, tiles(q, e, 0))

                def middle(q, e):
                    n0 = uses(q, e)
                    with act.Fori(1, NF) as i:
                        w1, w3, w2 = units(q, e, i)
                        split_hi(act, w1, 2, n0 + i - 1)
                        split_hi(act, w3, 0, n0 + i)
                        act_aT(act, 1, tiles(q, e, i - 1))
                        split_hi(act, w2, 1, n0 + i)
                        act_silu(act, 1, w1, tiles(q, e, i))

                def first_unit(q, e, n):
                    split_hi(act, U_MOE + U_PASS * q + 3 * NF * e + n, n, uses(q, e))

                def closing(q, e):
                    split_hi(act, units(q, e, NF)[0], 2, uses(q, e) + NF - 1)
                    if not (isinstance(e, int) and e == NE - 1):
                        first_unit(q, e + 1, 0)
                    act_aT(act, 1, tiles(q, e, NF - 1))

                def expert_out(q, e):
                    act.wait_ge(unit_used, U_MOE + U_PASS * q + 3 * NF * (e + 1))
                    for h in range(2):
                        act.copy(yhi[:, 4 * h:4 * h + 4, :], heads(Y[h])).then_inc(yhi_ready, 1)

                def moe(q):
                    gathered(NE * q)
                    first_unit(q, 0, 0)
                    first_unit(q, 0, 1)
                    opening_silu(q, 0)
                    with act.Fori(0, NE - 1) as e:
                        middle(q, e)
                        closing(q, e)
                        gathered(NE * q + e + 1)
                        first_unit(q, e + 1, 1)
                        expert_out(q, e)
                        opening_silu(q, e + 1)
                    middle(q, NE - 1)
                    closing(q, NE - 1)
                    expert_out(q, NE - 1)

                moe(0)
                act.wait_ge(flag_ready, 1)
                more = act.value_load(flag[0:1, 0:1], min_val=0, max_val=1)
                with act.If(more == 1):
                    moe(1)
                act.nop()

            @block.vector
            def _(dve):
                link = linker(dve, "dve", dve_step)
                dve_norm(dve, 3, link)
                lo_u(dve, U_ROUTER, KD * NE)
                lg, eq, idx, oh1, l2g, oh2, tmp, gate = lgt[0:8]
                it = iota[:, 0:NE]
                dve.wait_ge(unit_used, U_ROUTER + 1)
                link(dve.tensor_copy(lg, ps[4][:, 0:TT * NE].rearrange("p (t n) -> p t n", t=TT)))
                v = [sm(472 + 2 * n, TT) for n in range(4)]

                def best(x, value, index, onehot):
                    link(dve.tensor_reduce(value, x, AX.X, ALU.max))
                    link(dve.tensor_tensor(eq, x, along(value, NE), ALU.is_lt))
                    link(dve.scalar_tensor_tensor(tmp, eq, float(P), over_heads(it, TT), ALU.mult, ALU.add))
                    link(dve.tensor_reduce(index, tmp, AX.X, ALU.min))
                    link(dve.tensor_tensor(onehot, over_heads(it, TT), along(index, NE), ALU.is_equal))

                best(lg, v[0], v[1], oh1)
                link(dve.tensor_scalar(eq, oh1, -1.0, 1.0, ALU.mult, ALU.add))
                link(dve.tensor_tensor(l2g, lg, eq, ALU.mult))
                link(dve.scalar_tensor_tensor(l2g, oh1, -3.0e38, l2g, ALU.mult, ALU.add))
                best(l2g, v[2], v[3], oh2)
                e2 = lgt[13][:, :, 0]
                link(dve.tensor_tensor(e2, v[2], v[0], ALU.subtract))
                link(dve.tensor_copy(lgt[13][:, :, 1:NE], lg[:, :, 1:NE]))
                dve.tensor_scalar(lgt[13][:, :, 1:2], lgt[13][:, :, 0:1], 1.0, None, ALU.mult).then_inc(rt_in, 1)
                chosen = lgt[8]
                link(dve.tensor_tensor(chosen, oh1, oh2, ALU.add))
                dve.tensor_copy(eq, chosen).then_inc(rank_in, 1)
                dve.wait_ge(rt_exp, 1)
                link(dve.tensor_scalar(v[0], e2, 1.0, None, ALU.add))
                link(dve.reciprocal(v[0], v[0]))
                link(dve.tensor_tensor(v[1], e2, v[0], ALU.mult))
                link(dve.tensor_tensor(gate, oh1, along(v[0], NE), ALU.mult))
                link(dve.tensor_tensor(tmp, oh2, along(v[1], NE), ALU.mult))
                link(dve.memset(gates, 0.0))
                link(dve.tensor_tensor(gates[:, :, 0:NE], gate, tmp, ALU.add))
                dve.wait_ge(rank_ps, 1)
                rank = ps[5][:, 0:TT * NE].rearrange("p (t n) -> p t n", t=TT)
                link(dve.memset(slot_of, -1.0))
                link(dve.scalar_tensor_tensor(tmp, rank, 1.0, chosen, ALU.add, ALU.mult))
                link(dve.tensor_scalar(slot_of[:, :, 0:NE], tmp, -1.0, None, ALU.add))
                link(dve.tensor_reduce(cnt[:, 0:1], ps[5][:, 32:32 + NE], AX.X, ALU.max))
                dve.tensor_scalar(flag[0:1, 0:1], cnt[0:1, 0:1], float(CAP), None, ALU.is_gt).then_inc(flag_ready, 1)

                def select(q, e, n):
                    if not (isinstance(n, int) and n == 0):
                        dve.wait_ge(PT_ps, n)
                        dve.wait_ge(sel_ready, 2 * n)
                    link2(dve.tensor_copy(rcol, slot_of[:, :, bass.ds(e, 1)].rearrange("p t n -> p (t n)")), n)
                    for t in range(TT):
                        dve.tensor_scalar(slots_of(t), iota, float(CAP * q), rcol[:, t:t + 1], ALU.add,
                                          ALU.is_equal).then_inc(sel_ready, 1)

                def link2(ins, n):
                    ins.then_inc(rcol_ready, 1)
                    dve.wait_ge(rcol_ready, n + 1)

                def gathered(n):
                    for b in range(2):
                        dve.wait_ge(xghi_ready, 2 * n + b + 1)
                        dve.tensor_tensor(xglo[:, 4 * b:4 * b + 4, :], heads(GATHER[b]),
                                          xghi[:, 4 * b:4 * b + 4, :].bitcast(F32), ALU.subtract).then_inc(xglo_ready, 1)

                def turned(n):
                    dve.wait_ge(PT_ps, n + 1)
                    dve.tensor_copy(PT[:, :, :], TP[1][:, 0:TT * P].rearrange("p (t i) -> p t i", t=TT)).then_inc(PT_ready, 1)

                def opening_gate(q, e):
                    dve_gate(dve, 1, U_MOE + U_PASS * q + 3 * NF * e + 1, tiles(q, e, 0))

                def middle(q, e):
                    with dve.Fori(1, NF) as i:
                        w1, w3, w2 = units(q, e, i)
                        split_lo(dve, w3, 0)
                        dve_aT(dve, 1, tiles(q, e, i - 1))
                        split_lo(dve, w2, 1)
                        dve_gate(dve, 1, w3, tiles(q, e, i))
                        split_lo(dve, w2 + 1, 2)

                def expert_out(n):
                    for h in range(2):
                        dve.wait_ge(yhi_ready, 2 * n + h + 1)
                        dve.tensor_tensor(ylo[:, 4 * h:4 * h + 4, :], heads(Y[h]),
                                          yhi[:, 4 * h:4 * h + 4, :].bitcast(F32), ALU.subtract).then_inc(ylo_ready, 1)

                def scattered(e, n):
                    dve.tensor_copy(gcol, gates[:, :, bass.ds(e, 1)].rearrange("p t n -> p (t n)")).then_inc(gcol_ready, 1)
                    dve.wait_ge(gcol_ready, n + 1)
                    for j in range(4):
                        t, h = divmod(j, 2)
                        dve.wait_ge(sc_done, 4 * n + j + 1)
                        x = xres[:, t, h * GW:h * GW + GW]
                        dve.scalar_tensor_tensor(x, SCATTER[j][:, :], gcol[:, t:t + 1], x, ALU.mult,
                                                 ALU.add).then_inc(sc_added, 1)
                    dve.wait_ge(sc_added, 4 * n + 4)

                def moe(q):
                    n0 = NE * q
                    if q:
                        dve.wait_ge(out_sent, 16)
                    select(q, 0, n0)
                    gathered(n0)
                    split_lo(dve, U_MOE + U_PASS * q, 0)
                    split_lo(dve, U_MOE + U_PASS * q + 1, 1)
                    opening_gate(q, 0)
                    split_lo(dve, U_MOE + U_PASS * q + 2, 2)
                    turned(n0)
                    with dve.Fori(0, NE - 1) as e:
                        select(q, e + 1, n0 + e + 1)
                        middle(q, e)
                        u = U_MOE + U_PASS * q + 3 * NF * (e + 1)
                        split_lo(dve, u, 0, halves=(0,))
                        dve_aT(dve, 1, tiles(q, e, NF - 1))
                        split_lo(dve, u, 0, halves=(1,))
                        gathered(n0 + e + 1)
                        split_lo(dve, u + 1, 1)
                        expert_out(n0 + e)
                        split_lo(dve, u + 2, 2)
                        opening_gate(q, e + 1)
                        scattered(e, n0 + e)
                        turned(n0 + e + 1)
                    middle(q, NE - 1)
                    dve_aT(dve, 1, tiles(q, NE - 1, NF - 1))
                    expert_out(n0 + NE - 1)
                    scattered(NE - 1, n0 + NE - 1)

                moe(0)
                dve.wait_ge(flag_ready, 1)
                more = dve.value_load(flag[0:1, 0:1], min_val=0, max_val=1)
                with dve.If(more == 1):
                    moe(1)
                dve.nop()

            @block.tensor
            def _(pe):
                pe_norm(pe, 3)
                u = U_ROUTER
                for t in range(TT):
                    ins = tokens_by_columns(pe, u, ps[4][:, t * NE:t * NE + NE], t, n=NE)
                ins.then_inc(unit_used, 1)
                pe.wait_ge(rank_in, 1)
                chosen = lgt[8]
                pe.matmul(ps[5][:, 0:NE], strict, chosen[:, 0, :], start=True, stop=True)
                pe.matmul(ps[5][:, NE:2 * NE], strict, chosen[:, 1, :], start=True, stop=False)
                pe.matmul(ps[5][:, NE:2 * NE], ones, chosen[:, 0, :], start=False, stop=True)
                for t in range(TT):
                    ins = pe.matmul(ps[5][:, 32:32 + NE], ones, chosen[:, t, :], start=t == 0, stop=t == 1)
                ins.then_inc(rank_ps, 1)

                def gather(n):
                    pe.wait_ge(sel_ready, 2 * n + 2)
                    for k in range(KD):
                        for t in range(TT):
                            ins = pe.matmul(heads(GATHER[k // 4])[:, k % 4, :], xn[:, t, k * P:k * P + P],
                                            slots_of(t), start=t == 0, stop=t == 1)
                    ins.then_inc(xg_ps, 1)

                def turn_slots(n):
                    for t in range(TT):
                        ins = pe.transpose(TP[1][:, t * P:t * P + P], slots_of(t), ident)
                    ins.then_inc(PT_ps, 1)

                def opening(q, e):
                    u = U_MOE + U_PASS * q + 3 * NF * e
                    pe.wait_ge(xglo_ready, 2 * (NE * q + e) + 2)
                    pe_up(pe, u, 0, H1, 1, left=(xghi, xglo))
                    pe_up(pe, u + 1, 1, H3, 1, left=(xghi, xglo))

                def down_product(g, u, s, first, last):
                    pe.wait_ge(aTlo_ready, g + 1)
                    pe.wait_ge(lo_ready, 2 * u + 2)
                    for h in range(2):
                        ins = down(pe, Y[h][:, :], 0, s, h, first, last)
                    ins.then_inc(unit_used, 1)

                def step(q, e, i, first):
                    w1, w3, w2 = units(q, e, i)
                    pe.wait_ge(sil_ready, tiles(q, e, i))
                    pe_up(pe, w1, 2, H1, 1, left=(xghi, xglo))
                    pe_up(pe, w3, 0, H3, 1, left=(xghi, xglo))
                    down_product(tiles(q, e, i - 1), w2, 1, first, False)
                    pe_turn(pe, 1, tiles(q, e, i))

                def middle(q, e):
                    step(q, e, 1, True)
                    with pe.Fori(2, NF) as i:
                        step(q, e, i, False)

                def scatter(n):
                    pe.wait_ge(ylo_ready, 2 * n + 2)
                    pe.wait_ge(PT_ready, n + 1)
                    for j in range(4):
                        t, h = divmod(j, 2)
                        to = SCATTER[j][:, :]
                        pe.matmul(to, PT[:, t, :], yhi[:, 4 * h:4 * h + 4, :], start=True, stop=False)
                        pe.matmul(to, PT[:, t, :], ylo[:, 4 * h:4 * h + 4, :], start=False, stop=True).then_inc(sc_done, 1)

                def moe(q):
                    n0 = NE * q
                    gather(n0)
                    opening(q, 0)
                    pe_turn(pe, 1, tiles(q, 0, 0))
                    turn_slots(n0)
                    with pe.Fori(0, NE - 1) as e:
                        middle(q, e)
                        gather(n0 + e + 1)
                        down_product(tiles(q, e, NF - 1), U_MOE + U_PASS * q + 3 * NF * (e + 1) - 1, 2, False, True)
                        opening(q, e + 1)
                        scatter(n0 + e)
                        pe_turn(pe, 1, tiles(q, e + 1, 0))
                        turn_slots(n0 + e + 1)
                    middle(q, NE - 1)
                    down_product(tiles(q, NE - 1, NF - 1), U_MOE + U_PASS * (q + 1) - 1, 2, False, True)
                    scatter(n0 + NE - 1)

                moe(0)
                pe.wait_ge(flag_ready, 1)
                more = pe.value_load(flag[0:1, 0:1], min_val=0, max_val=1)
                with pe.If(more == 1):
                    moe(1)
                pe.nop()


_INS = ["x", "ev_norm1", "ev_w_in", "ev_w_out", "ev_norm2", "ev_ffn_w1", "ev_ffn_w3", "ev_ffn_w2",
        "od_norm1", "od_w_in", "od_w_out", "od_norm2", "od_router", "od_moe_w1", "od_moe_w3", "od_moe_w2"]


def layout(inputs):
    arrays = {n: np.ascontiguousarray(inputs[n]) for n in _INS}
    row = lambda v: np.broadcast_to(np.asarray(v).reshape(1, -1), (P, np.asarray(v).size))
    arrays["params"] = np.ascontiguousarray(np.concatenate([
        row(inputs["ev_a_log"]), row(inputs["ev_dt_bias"]), np.asarray(inputs["ev_o_norm"]).reshape(P, 1),
        np.zeros((P, 3), np.float32),
        np.asarray(inputs["ev_conv_qkv"])[0].reshape(4, 3 * H, P).transpose(2, 1, 0).reshape(P, 12 * H),
        np.asarray(inputs["ev_conv_sc"])[0].reshape(3, H, P).transpose(2, 1, 0).reshape(P, 3 * H),
        row(inputs["od_q_norm"]), row(inputs["od_k_norm"]), row(inputs["od_sinks"])], axis=1))
    arrays["consts"] = constants()
    return arrays


def kernel(**inputs):
    import concourse.bacc as bacc
    from concourse.bass_utils import run_bass_kernel_spmd

    nc = bacc.Bacc("TRN2", target_bir_lowering=False, num_devices=1, dynamic_dma_scratch_size=1024)
    arrays = layout(inputs)
    aps = {n: nc.dram_tensor(f"in_{n}", v.shape, F32, kind="ExternalInput").ap() for n, v in arrays.items()}
    out = nc.dram_tensor("out", (1, T, D), F32, kind="ExternalOutput").ap()
    build_program(nc, aps, out)
    r = run_bass_kernel_spmd(nc, [{f"in_{n}": v for n, v in arrays.items()}], core_ids=[0])
    return r.results[0]["out"]
```

```python
from contextlib import ExitStack

import numpy as np

import concourse.bass as bass
from concourse import mybir

F32 = mybir.dt.float32
F32R = mybir.dt.float32r
I32 = mybir.dt.int32
ALU = mybir.AluOpType
ACT = mybir.ActivationFunctionType
AX = mybir.AxisListType

P = 128
D = 1024
T = 256
TT = T // P
KD = D // P
H = 4
GW = 512
F = 3584
NF = F // GW
FC = GW // P
NE = 8
CAP = P
QH, KVH, HD = 16, 2, 64
GRP = QH // KVH
UNIT = KD * GW
HALF = UNIT // 2
NS = 3
EPS = 1e-6
NEG = -1e30
LEVELS = 7

U_Q, U_K, U_V, U_CG, U_XIN, U_BG, U_Z, U_OUT0, U_FFN = 0, 1, 2, 3, 4, 5, 6, 7, 9
U_IN1 = U_FFN + 3 * NF
U_OUT1 = U_IN1 + 3
U_ROUTER = U_OUT1 + 2
U_MOE = U_ROUTER + 1
U_PASS = 3 * NF * NE
EVEN_COL = {U_Q: 0, U_K: 512, U_V: 1024, U_Z: 1536, U_BG: 2056, U_CG: 2568, U_XIN: 3080}

C_ID, C_UI, C_US, C_ONE, C_IOTA, C_MAIN = 0, 128, 256, 384, 512, 640
C_LEV = C_MAIN
C_MASK = C_LEV + LEVELS * P
C_ALL = C_MASK + 2 * P
ARENA = 10304


def constants():
    i = np.arange(P)
    c = np.zeros((P, C_ALL), np.float32)
    c[:, C_ID:C_ID + P] = np.eye(P)
    c[:, C_UI:C_UI + P] = i[:, None] <= i[None, :]
    c[:, C_US:C_US + P] = i[:, None] < i[None, :]
    c[:, C_ONE:C_ONE + P] = 1.0
    c[:, C_IOTA:C_IOTA + P] = i[None, :]
    for n in range(LEVELS):
        b = 1 << n
        same = lambda w: (i[:, None] // w) == (i[None, :] // w)
        c[:, C_LEV + n * P:C_LEV + (n + 1) * P] = same(2 * b) & ~same(b)
    c[:, C_MASK:C_MASK + P] = np.where(i[None, :] > i[:, None], 0.0, NEG)
    c[:, C_MASK + P:C_MASK + 2 * P] = np.where(i[None, :] <= i[:, None], 0.0, NEG)
    return c


def band(t, k, n):
    return t[:, 0:k * n].rearrange("p (k n) -> p k n", k=k)


def build_program(nc, a, out):
    with ExitStack() as ctx:
        def sb(name, shape, dt=F32):
            return ctx.enter_context(nc.sbuf_tensor(name, shape, dt))

        def sem(names):
            return [ctx.enter_context(nc.semaphore(n)) for n in names.split()]

        raw = [sb(f"raw{s}", [P, UNIT]) for s in range(NS)]
        whi = [sb(f"whi{s}", [P, UNIT], F32R) for s in range(NS)]
        wlo = [sb(f"wlo{s}", [P, UNIT], F32R) for s in range(NS)]
        xres = sb("xres", [P, TT, D])
        hThi = sb("hThi", [P, KD, T], F32R)
        hTlo = sb("hTlo", [P, KD, T], F32R)
        aThi = sb("aThi", [P, TT, FC, P], F32R)
        aTlo = sb("aTlo", [P, TT, FC, P], F32R)
        PT = sb("PT", [P, TT, P], F32R)
        cst = sb("cst", [P, C_MAIN])
        small = sb("small", [P, 480])
        flag = sb("flag", [1, 2], I32)
        arena = sb("arena", [P, ARENA])

        ident, upper, strict, ones, iota = (cst[:, c:c + P] for c in (C_ID, C_UI, C_US, C_ONE, C_IOTA))

        def view(t, at, *shape):
            v = t[:, at:at + int(np.prod(shape))]
            if len(shape) == 1:
                return v
            names = "abcd"[:len(shape)]
            return v.rearrange(f"p ({' '.join(names)}) -> p {' '.join(names)}",
                               **{k: s for k, s in zip(names[1:], shape[1:])})

        def ar(at, *shape):
            return view(arena, at, *shape)

        def sm(at, *shape):
            return view(small, at, *shape)

        def over_heads(x, n=H):
            return x.unsqueeze(1).to_broadcast([P, n, x.shape[1]])

        def along(x, n):
            return x.unsqueeze(2).to_broadcast([P, x.shape[1], n])

        xn = ar(0, TT, D)
        gain = ar(2048, D)
        Q, K, V = ar(0, H, T), ar(1024, H, T), ar(2048, H, T)
        conv_in = [ar(3072 + H * (3 + T) * n, H, 3 + T) for n in range(3)]
        sq = [ar(6180, H, T), ar(3072, H, T)]
        KN = ar(3072, 2, H, P)
        Vn = ar(4096, TT, H, P)
        attnT = view(raw[0], 0, TT, H, P)
        Achunk = view(raw[0], TT * GW, TT, H, P)
        zs = ar(6180, H, T)
        ysc = ar(7204, H, T)
        cgx = ar(8228, H, 2 + T)
        osq = ar(8228, 2, GW)
        S1 = ar(1024, H, P)
        wT = ar(1536, H, P)
        lev = xres[:, 0, 0:LEVELS * P].rearrange("p (n i) -> p n i", i=P)
        rowbuf = [xres[:, 1, n * GW:(n + 1) * GW].rearrange("p (h i) -> p h i", h=H) for n in range(2)]
        Tm, Bm = (ar(8228, H, P), ar(2048, H, P)), (ar(8740, H, P), ar(2560, H, P))
        Aoff, M1 = (ar(9252, H, P), ar(5120, H, P)), (ar(9764, H, P), rowbuf[0])
        eG = ar(5632, H, P)
        rr = sm(320, 2, TT, H)
        bk, so, so2, om, orr = (sm(336 + 8 * n, TT, H) for n in range(5))
        qkv = ar(0, TT, D + 2 * KVH * HD)
        qT = ar(2560, KD, T)
        kdup = ar(4608, TT, KVH, 2, HD)
        kT = ar(5120, KVH, T)
        masks = ar(5632, 2, P)
        hsq = ar(5888, TT, QH + KVH, HD)
        prob = [ar(5888 + 1024 * n, 1024) for n in range(2)]
        probT = [ar(7936 + 1024 * n, 8, P) for n in range(2)]
        sil = ar(2048, TT, GW)
        actf = ar(3072, TT, GW)
        Psel = ar(4096, TT, P)
        lgt = [ar(4352 + 16 * n, TT, NE) for n in range(14)]
        slot_of = ar(4576, TT, NE + 1)
        gates = ar(4594, TT, NE + 1)
        xghi, xglo = hThi[:, :, 0:P], hTlo[:, :, 0:P]
        yhi, ylo = hThi[:, :, P:T], hTlo[:, :, P:T]

        ss, rs = sm(0, TT), sm(2, TT)
        wabhi, wablo = sb("wabhi", [P, KD * 2 * H], F32R), sb("wablo", [P, KD * 2 * H], F32R)
        wab = ar(9400, KD * 2 * H)
        beta, gdec, Gc = sm(24, TT, H), sm(32, TT, H), sm(40, TT, H)
        pre, ey, eb, t4, t5, t6 = (sm(48 + 8 * n, TT, H) for n in range(6))
        kd, kg = sm(96, H), sm(100, H)
        alog, dtb, onorm = sm(104, H), sm(108, H), sm(112, 1)
        convw, scw = sm(116, 3 * H, 4), sm(164, H, 3)
        qnw, knw, sinks = sm(176, HD), sm(240, HD), sm(304, QH)
        hss = sm(320, TT, QH + KVH)
        hrs = sm(356, TT, QH + KVH)
        smax, nmax, rsum, esink = ((sm(392 + 16 * n, QH), sm(24 + 16 * n, QH)) for n in range(4))
        rcol, gcol, cnt = sm(456, TT), sm(458, TT), sm(460, NE)

        ps = [ctx.enter_context(nc.psum_tensor(f"ps{n}", [P, GW], F32)) for n in range(8)]
        H1, H3, TP, Y = ps[0:2], ps[2:4], ps[4:6], ps[6:8]

        def heads(t):
            return t[:, :].rearrange("p (h i) -> p h i", i=P)

        def pairs(t):
            return t[:, :].rearrange("p (k t) -> p k t", k=2)

        raw_full = sem("raw_full0 raw_full1 raw_full2")
        hi_ready, lo_ready, unit_used = sem("hi_ready lo_ready unit_used")
        dve_step, = sem("dve_step")
        x_in, cst_in, par_in, wab_in, lev_in, gain_in, x_again, mask_in = sem(
            "x_in cst_in par_in wab_in lev_in gain_in x_again mask_in")
        n_sq, n_ms, n_rt, xn_ready, hT_ps, hThi_ready, hT_ready = sem(
            "n_sq n_ms n_rt xn_ready hT_ps hThi_ready hT_ready")
        out_ps, out_added = sem("out_ps out_added")
        sil_ready, a_ready, aT_ps, aThi_ready, aTlo_ready, y_done, y_added = sem(
            "sil_ready a_ready aT_ps aThi_ready aTlo_ready y_done y_added")
        steps = {"dve": 0}

        def linker(dve):
            def link(ins):
                steps["dve"] += 1
                ins.then_inc(dve_step, 1)
                dve.wait_ge(dve_step, steps["dve"])
            return link

        def load(sp, u, s, dst, src):
            if not (isinstance(u, int) and u < NS):
                sp.wait_ge(lo_ready, 2 * (u - NS + 1))
            sp.dma_start(dst, src).then_inc(raw_full[s], 16)

        def split_hi(act, u, s, n, size=UNIT):
            act.wait_ge(raw_full[s], 16 * (n + 1))
            if not (isinstance(u, int) and u < NS):
                act.wait_ge(unit_used, u - NS + 1)
            for h in range(2):
                part = slice(h * size // 2, (h + 1) * size // 2)
                act.copy(whi[s][:, part], raw[s][:, part]).then_inc(hi_ready, 1)

        def split_lo(dve, u, s, size=UNIT, halves=(0, 1)):
            for h in halves:
                part = slice(h * size // 2, (h + 1) * size // 2)
                dve.wait_ge(hi_ready, 2 * u + h + 1)
                dve.tensor_tensor(wlo[s][:, part], raw[s][:, part], whi[s][:, part].bitcast(F32),
                                  ALU.subtract).then_inc(lo_ready, 1)

        def hi_u(act, u, size=UNIT):
            split_hi(act, u, u % NS, u // NS, size)

        def lo_u(dve, u, size=UNIT):
            split_lo(dve, u, u % NS, size)

        def product(pe, to, lhi, llo, rhi, rlo, first, last):
            pe.matmul(to, lhi, rhi, start=first, stop=False)
            pe.matmul(to, lhi, rlo, start=False, stop=False)
            return pe.matmul(to, llo, rhi, start=False, stop=last)

        def tokens_by_columns(pe, u, to, tile, n=GW, s=None, left=None, fresh=None):
            s = u % NS if s is None else s
            lh, ll = left or (hThi[:, :, tile * P:tile * P + P], hTlo[:, :, tile * P:tile * P + P])
            wh, wl = band(whi[s], KD, n), band(wlo[s], KD, n)
            for k in range(KD):
                if fresh is not None and k % 2 == 0 and tile == 0:
                    pe.wait_ge(hT_ready, 4 * fresh + k // 2 + 1)
                if k % 4 == 0 and tile == 0:
                    pe.wait_ge(lo_ready, 2 * u + k // 4 + 1)
                ins = product(pe, to, lh[:, k], ll[:, k], wh[:, k], wl[:, k], k == 0, k == KD - 1)
            return ins

        def act_square(act, t, src):
            act.wait_ge(src[0], src[1])
            act.activation(xn[:, t, :], xres[:, t, :], ACT.Square, accum_out=ss[:, t:t + 1]).then_inc(n_sq, 1)

        def act_norm(act, n, src, between=()):
            for t in range(1 if n else 0, TT):
                act_square(act, t, src)
            act.wait_ge(n_ms, n + 1)
            act.activation(rs, ss, ACT.Sqrt).then_inc(n_rt, 1)
            for work in between:
                work()
            for b in range(4):
                act.wait_ge(hT_ps, 4 * n + b + 1)
                act.copy(hThi[:, 2 * b:2 * b + 2, :], pairs(ps[b])).then_inc(hThi_ready, 1)

        def dve_norm(dve, n, link, before=(), between=()):
            for work in before:
                work()
            dve.wait_ge(n_sq, TT * (n + 1))
            dve.tensor_scalar(ss, ss, 1.0 / D, EPS, ALU.mult, ALU.add).then_inc(n_ms, 1)
            dve.wait_ge(n_rt, n + 1)
            link(dve.reciprocal(rs, rs))
            dve.wait_ge(gain_in, 16 * (n + 1))
            for t in range(TT):
                dve.scalar_tensor_tensor(xn[:, t, :], xres[:, t, :], rs[:, t:t + 1], gain, ALU.mult,
                                         ALU.mult).then_inc(xn_ready, 1)
            for work in between:
                work()
            dve_transposed(dve, 4 * n)

        def dve_transposed(dve, n0):
            for b in range(4):
                dve.wait_ge(hThi_ready, n0 + b + 1)
                dve.tensor_tensor(hTlo[:, 2 * b:2 * b + 2, :], pairs(ps[b]),
                                  hThi[:, 2 * b:2 * b + 2, :].bitcast(F32), ALU.subtract).then_inc(hT_ready, 1)

        def pe_norm(pe, n):
            for t in range(TT):
                pe.wait_ge(xn_ready, TT * n + t + 1)
                for k in range(KD):
                    ins = pe.transpose(pairs(ps[k // 2])[:, k % 2, t * P:t * P + P],
                                       xn[:, t, k * P:k * P + P], ident)
                    if k % 2 and t == TT - 1:
                        ins.then_inc(hT_ps, 1)

        def even_unit(u):
            if u < U_OUT0:
                return band(raw[u % NS], KD, GW), column_block(a["ev_w_in"][0], EVEN_COL[u])
            return band(raw[u % NS], KD, GW), column_block(a["ev_w_out"][0], (u - U_OUT0) * GW)

        def column_block(w, c0, n=GW):
            return w.rearrange("(k p) n -> p k n", p=P)[:, :, c0:c0 + n]

        def odd_unit(u):
            if u == U_ROUTER:
                return band(raw[u % NS], KD, NE), column_block(a["od_router"][0], 0, NE)
            w, c = ("od_w_in", (u - U_IN1 + 2) % 3) if u < U_OUT1 else ("od_w_out", u - U_OUT1)
            n = GW if u != U_IN1 else GW // 2
            return band(raw[u % NS], KD, n), column_block(a[w][0], c * GW, n)

        w1f, w3f = (a[n][0].rearrange("(k p) n -> p k n", p=P) for n in ("ev_ffn_w1", "ev_ffn_w3"))
        w2f = a["ev_ffn_w2"][0].rearrange("(b c p) n -> b p c n", p=P, c=FC)
        w1m, w3m = (a[n][0].rearrange("e (k p) n -> e p k n", p=P) for n in ("od_moe_w1", "od_moe_w3"))
        w2m = a["od_moe_w2"][0].rearrange("e (b c p) n -> (e b) p c n", p=P, c=FC)

        def ffn_col(w):
            return lambda i: w[:, :, bass.ds(i * GW, GW)]

        def moe_col(w, e):
            return lambda i: w[bass.ds(e, 1), :, :, bass.ds(i * GW, GW)].rearrange("e p k n -> p (e k) n")

        ffn_down = lambda i: w2f[bass.ds(i, 1)].rearrange("b p c n -> p (b c) n")

        def moe_down(e):
            return lambda i: w2m[bass.ds(e * NF + i, 1)].rearrange("b p c n -> p (b c) n")

        def first_loads(sp, u0, w1, w3, order=(0, 1, 2)):
            for n in order:
                load(sp, u0 + n, n, band(raw[n], KD, GW), (w1(0), w3(0), w1(1))[n])
                if order[0] and n == 2:
                    sp.wait_ge(o_ps, 2)

        def swiglu_loads(sp, u0, w1, w3, w2):
            load(sp, u0 + 3, 0, band(raw[0], KD, GW), w3(1))
            load(sp, u0 + 4, 1, band(raw[1], FC, D), w2(0))
            with sp.Fori(2, NF) as i:
                load(sp, u0 + 3 * i - 1, 2, band(raw[2], KD, GW), w1(i))
                load(sp, u0 + 3 * i, 0, band(raw[0], KD, GW), w3(i))
                load(sp, u0 + 3 * i + 1, 1, band(raw[1], FC, D), w2(i - 1))
            load(sp, u0 + 3 * NF - 1, 2, band(raw[2], FC, D), w2(NF - 1))

        def act_silu(act, tiles, u, g):
            act.wait_ge(unit_used, u + 1)
            if not (isinstance(g, int) and g == 0):
                act.wait_ge(a_ready, g)
            for t in range(tiles):
                act.activation(sil[:, t, :], H1[t][:, :], ACT.Silu).then_inc(sil_ready, 1)

        def act_aT(act, g):
            act.wait_ge(aT_ps, g - 2 * NF + 1)
            act.copy(aThi[:, 0], heads(TP[0])).then_inc(aThi_ready, 1)

        def dve_gate(dve, tiles, u, g):
            dve.wait_ge(unit_used, u + 1)
            for t in range(tiles):
                dve.wait_ge(sil_ready, g + t + 1)
                dve.tensor_tensor(actf[:, t, :], sil[:, t, :], H3[t][:, :], ALU.mult).then_inc(a_ready, 1)

        def dve_aT(dve, g):
            dve.wait_ge(aThi_ready, g + 1)
            dve.tensor_tensor(aTlo[:, 0], heads(TP[0]), aThi[:, 0].bitcast(F32), ALU.subtract).then_inc(aTlo_ready, 1)

        def pe_up(pe, u, s, to):
            tokens_by_columns(pe, u, to[:, :], 0, s=s, left=(xghi, xglo)).then_inc(unit_used, 1)

        def pe_turn(pe, g):
            pe.wait_ge(a_ready, g + 1)
            for c in range(FC):
                ins = pe.transpose(TP[0][:, c * P:c * P + P], actf[:, 0, c * P:c * P + P], ident)
            ins.then_inc(aT_ps, 1)

        def down(pe, to, s, half, first, last):
            wh, wl = band(whi[s], FC, D), band(wlo[s], FC, D)
            n = slice(half * GW, half * GW + GW)
            for c in range(FC):
                ins = product(pe, to, aThi[:, 0, c], aTlo[:, 0, c], wh[:, c, n], wl[:, c, n],
                              first and c == 0, last and c == FC - 1)
            return ins
        (pads, wab_hi, wab_lo, ab_done, proj_taken, gates_in, gates_exp, g_ready, gc_ps,
         conv_done, silu_done, l2_sq, l2_ps, l2_ms, l2_rt, row_ready, row_ps, eG_ready,
         diff_ready, dec_exp, nat_ps, nat_ready, kk_ps, kk_taken, qdec_ready, tri_init, aoff_ready,
         m1_ps, m1_ready, upd_ps, T_ready, B_ready, u_ps, u_ready, s1_ps, s1_ready, ws_ps, vnew_ready,
         o_ps, o_sq, o_ssq, o_ms, o_rt, mix_ready, mix_hi, mix_lo) = sem(
            "pads wab_hi wab_lo ab_done proj_taken gates_in gates_exp g_ready gc_ps "
            "conv_done silu_done l2_sq l2_ps l2_ms l2_rt row_ready row_ps eG_ready "
            "diff_ready dec_exp nat_ps nat_ready kk_ps kk_taken qdec_ready tri_init aoff_ready "
            "m1_ps m1_ready upd_ps T_ready B_ready u_ps u_ready s1_ps s1_ready ws_ps vnew_ready "
            "o_ps o_sq o_ssq o_ms o_rt mix_ready mix_hi mix_lo")
        PROJ = [ps[4:6], ps[6:8], ps[0:2]]
        O = [ps[4], ps[6]]
        ab_chan = ar(9400 + KD * 2 * H, T)[0:2 * H]
        ab_rows, = sem("ab_rows")
        BANKS = [0, 1, 0, 1, 0, 1, 2]
        PAIR = [slice(0, 2), slice(2, 4)]
        NAT = [4, 5, 2, 3]
        BLOCKS = [(t, b) for t in range(TT) for b in range(2)]
        brow_taken, tap_ready = sem("brow_taken tap_ready")

        with nc.Block() as block:
            @block.sync
            def _(sp):
                sp.dma_start(xres[:, :, :], a["x"][0].rearrange("(t p) d -> p t d", p=P)).then_inc(x_in, 16)
                sp.dma_start(gain, a["ev_norm1"].to_broadcast([P, D])).then_inc(gain_in, 16)
                for u in range(U_FFN):
                    load(sp, u, u % NS, *even_unit(u))
                first_loads(sp, U_FFN, ffn_col(w1f), ffn_col(w3f), order=(1, 2, 0))

            @block.scalar
            def _(act):
                act.dma_start(cst[:, :], a["consts"][:, 0:C_MAIN]).then_inc(cst_in, 16)
                act.dma_start(wab.rearrange("p (k n) -> p k n", k=KD),
                              column_block(a["ev_w_in"][0], 4 * GW, 2 * H)).then_inc(wab_in, 16)
                act.dma_start(small[:, 104:320], a["params"]).then_inc(par_in, 16)
                act_norm(act, 0, (x_in, 16))
                act.wait_ge(wab_in, 16)
                act.copy(wabhi[:, :], wab).then_inc(wab_hi, 1)
                for u in (U_Q, U_K, U_V):
                    hi_u(act, u)
                act.wait_ge(xn_ready, 2)
                act.dma_start(lev, a["consts"][:, C_LEV:C_MASK].rearrange("p (n i) -> p n i", i=P)).then_inc(lev_in, 16)

                def take(n, dst):
                    act.wait_ge(unit_used, n + 1)
                    for b in range(2):
                        act.copy(dst[:, PAIR[b], :], pairs(PROJ[BANKS[n]][b])).then_inc(proj_taken, 1)

                act.wait_ge(gates_in, 1)
                act.activation(ey, ey, ACT.Exp).then_inc(gates_exp, 1)
                act.activation(eb, eb, ACT.Exp).then_inc(gates_exp, 1)
                act.activation(alog, alog, ACT.Exp).then_inc(gates_exp, 1)
                act.wait_ge(pads, 1)
                act.wait_ge(par_in, 16)
                for n in range(3):
                    take(n, conv_in[n][:, :, 3:3 + T])
                    act.wait_ge(proj_taken, 2 * n + 2)
                    for c in range(H):
                        act.activation((Q, K, V)[n][:, c, :], conv_in[n][:, c, 0:T], ACT.Copy,
                                       scale=convw[:, H * n + c, 0:1]).then_inc(tap_ready, 1)
                    hi_u(act, U_CG + n)
                take(3, cgx[:, :, 2:2 + T])
                hi_u(act, U_Z)
                for n, x in enumerate((Q, K)):
                    act.wait_ge(conv_done, n + 1)
                    act.activation(x, x, ACT.Silu).then_inc(silu_done, 1)
                for n, x in enumerate((Q, K)):
                    act.wait_ge(silu_done, n + 1)
                    act.activation(sq[n], x, ACT.Square).then_inc(l2_sq, 1)
                act.wait_ge(conv_done, 3)
                act.activation(V, V, ACT.Silu).then_inc(silu_done, 1)
                act.wait_ge(l2_ms, 1)
                act.activation(rr, rr, ACT.Sqrt).then_inc(l2_rt, 1)
                for t in range(TT):
                    act.wait_ge(diff_ready, t + 1)
                    act.activation(attnT[:, t], attnT[:, t], ACT.Exp).then_inc(dec_exp, 1)
                act.activation(kd, kd, ACT.Exp).then_inc(dec_exp, 1)
                act.activation(kg, Gc[:, 1, :], ACT.Exp).then_inc(dec_exp, 1)
                act.activation(eG, heads(ps[3]), ACT.Exp).then_inc(eG_ready, 1)
                for u in (U_OUT0, U_OUT0 + 1):
                    hi_u(act, u)
                act.wait_ge(unit_used, 7)
                for b in range(2):
                    act.activation(zs[:, PAIR[b], :], pairs(PROJ[2][b]), ACT.Silu).then_inc(proj_taken, 1)
                for t, b in BLOCKS:
                    act.wait_ge(tri_init, 2 * t + b + 1)
                    act.copy(Tm[t][:, PAIR[b]], heads(ps[4 + 2 * t + b])[:, PAIR[0]]).then_inc(T_ready, 1)
                for n in range(1, LEVELS):
                    for t, b in BLOCKS:
                        act.wait_ge(m1_ps, 4 * (n - 1) + 2 * t + b + 1)
                        act.copy(M1[t][:, PAIR[b]], heads(ps[2 * t + b])[:, PAIR[0]]).then_inc(m1_ready, 1)
                act.wait_ge(u_ps, 1)
                act.copy(Vn[:, 0], heads(ps[0])).then_inc(u_ready, 1)
                act.wait_ge(u_ps, 3)
                act.copy(wT, heads(ps[2])).then_inc(u_ready, 1)
                act.wait_ge(s1_ps, 1)
                act.copy(S1, heads(ps[3])).then_inc(s1_ready, 1)
                for t in range(TT):
                    act.wait_ge(o_ps, t + 1)
                    act.activation(osq[:, t, :], O[t][:, :], ACT.Square).then_inc(o_sq, 1)
                    act.wait_ge(o_ms, t + 1)
                    act.activation(om[:, t, :], om[:, t, :], ACT.Sqrt).then_inc(o_rt, 1)
                act.wait_ge(row_ps, 6)
                act.dma_start(xres[:, :, :], a["x"][0].rearrange("(t p) d -> p t d", p=P)).then_inc(x_again, 16)
                act.wait_ge(mix_ready, 2)
                for n, x in enumerate((Q, ysc)):
                    act.copy(hThi[:, 4 * n:4 * n + 4, :], x).then_inc(mix_hi, 1)
                act.dma_start(gain, a["ev_norm2"].to_broadcast([P, D])).then_inc(gain_in, 16)
                for u in (U_FFN, U_FFN + 1):
                    hi_u(act, u)
                act_square(act, 0, (out_added, 3))

            @block.vector
            def _(dve):
                link = linker(dve)
                for n in range(3):
                    dve.memset(conv_in[n][:, :, 0:3], 0.0)
                dve.memset(cgx[:, :, 0:2], 0.0).then_inc(pads, 1)
                dve_norm(dve, 0, link)
                dve.wait_ge(wab_hi, 1)
                dve.tensor_tensor(wablo[:, :], wab, wabhi[:, :].bitcast(F32), ALU.subtract).then_inc(wab_lo, 1)
                lo_u(dve, U_Q)
                dve.wait_ge(ab_done, 1)
                dve.tensor_copy(ab_chan, ps[1][0:2 * H, 0:T]).then_inc(ab_rows, 1)
                lo_u(dve, U_K)
                dve.wait_ge(ab_done, 2)
                dve.wait_ge(par_in, 16)
                ab = ps[0][:, 0:4 * H].rearrange("p (t n) -> p t n", t=TT)
                link(dve.tensor_tensor(pre, ab[:, :, 0:H], over_heads(dtb, TT), ALU.add))
                link(dve.tensor_scalar(t4, pre, -1.0, None, ALU.mult))
                link(dve.tensor_tensor(ey, pre, t4, ALU.min))
                dve.tensor_scalar(eb, ab[:, :, H:2 * H], -1.0, None, ALU.mult).then_inc(gates_in, 1)
                lo_u(dve, U_V)
                dve.wait_ge(gates_exp, 3)
                link(dve.tensor_scalar(t4, ey, 2.0, None, ALU.add))
                link(dve.reciprocal(t4, t4))
                link(dve.tensor_tensor(t4, t4, ey, ALU.mult))
                link(dve.tensor_tensor(t5, t4, t4, ALU.mult))
                link(dve.tensor_scalar(t6, t5, 1.0 / 19, None, ALU.mult))
                for n in range(8, 0, -1):
                    link(dve.scalar_tensor_tensor(t6, t6, 1.0 / (2 * n + 1), t5, ALU.add, ALU.mult))
                link(dve.scalar_tensor_tensor(t6, t6, 1.0, t4, ALU.add, ALU.mult))
                link(dve.tensor_scalar(pre, pre, 0.0, None, ALU.max))
                link(dve.scalar_tensor_tensor(t6, t6, 2.0, pre, ALU.mult, ALU.add))
                link(dve.scalar_tensor_tensor(gdec, t6, -1.0, over_heads(alog, TT), ALU.mult, ALU.mult))
                link(dve.tensor_scalar(eb, eb, 1.0, None, ALU.add))
                dve.reciprocal(beta, eb).then_inc(g_ready, 1)
                dve.wait_ge(gc_ps, 1)
                dve.wait_ge(g_ready, 1)
                link(dve.tensor_copy(Gc, ps[0][:, 32:32 + 2 * H].rearrange("p (t n) -> p t n", t=TT)))
                lo_u(dve, U_CG)

                def row(n, src, tri):
                    dve.tensor_tensor(rowbuf[n % 2], over_heads(tri), along(src, P), ALU.mult).then_inc(row_ready, 1)

                for t in range(TT):
                    row(t, gdec[:, t, :], upper)

                def conv(dst, src, w, taps):
                    if taps == 3:
                        for c in range(H):
                            dve.tensor_scalar(dst[:, c, :], src[:, c, 0:T], w[:, c, 0:1], None, ALU.mult).then_inc(dve_step, 1)
                        steps["dve"] += H
                        dve.wait_ge(dve_step, steps["dve"])
                    for j in range(1, taps):
                        for c in range(H):
                            ins = dve.scalar_tensor_tensor(dst[:, c, :], src[:, c, j:j + T], w[:, c, j:j + 1],
                                                           dst[:, c, :], ALU.mult, ALU.add)
                            if j < taps - 1:
                                ins.then_inc(dve_step, 1)
                        if j < taps - 1:
                            steps["dve"] += H
                            dve.wait_ge(dve_step, steps["dve"])
                    return ins

                for n, x in enumerate((Q, K, V)):
                    dve.wait_ge(tap_ready, H * n + H)
                    conv(x, conv_in[n], convw[:, H * n:H * n + H], 4).then_inc(conv_done, 1)
                    if n < 2:
                        lo_u(dve, U_XIN + n)
                dve.wait_ge(proj_taken, 8)
                dve.wait_ge(unit_used, 5)
                for b in range(2):
                    x = cgx[:, PAIR[b], 2:2 + T]
                    dve.tensor_tensor(x, x, pairs(PROJ[0][b]), ALU.mult).then_inc(proj_taken, 1)
                lo_u(dve, U_Z)
                dve.wait_ge(l2_ps, 1)
                dve.tensor_scalar(rr, ps[0][:, 64:64 + 4 * H].rearrange("p (a t h) -> p a t h", a=2, t=TT), EPS, None,
                                  ALU.add).then_inc(l2_ms, 1)
                dve.wait_ge(lo_ready, 2 * U_Z + 2)
                for t in range(TT):
                    dve.wait_ge(row_ps, t + 1)
                    link(dve.tensor_tensor(attnT[:, t], heads(ps[2 + t]), along(Gc[:, t, :], P), ALU.subtract))
                    if t == 0:
                        link(dve.tensor_tensor(kd, heads(ps[2])[:, :, P - 1], Gc[:, 0, :], ALU.subtract))
                    dve.tensor_scalar(attnT[:, t], attnT[:, t], 0.0, None, ALU.min).then_inc(diff_ready, 1)
                dve.wait_ge(l2_rt, 1)
                link(dve.reciprocal(rr, rr))
                rq, rk = rr[:, 0], rr[:, 1]
                link(dve.tensor_tensor(bk, beta, rk, ALU.mult))
                for t in range(TT):
                    row(t, bk[:, t, :], ident)
                dve.wait_ge(proj_taken, 10)
                link(conv(ysc, cgx, scw, 3))
                dve.wait_ge(unit_used, 6)
                for b in range(2):
                    x = ysc[:, PAIR[b], :]
                    dve.tensor_tensor(x, x, pairs(PROJ[1][b]), ALU.mult).then_inc(proj_taken, 1)
                dve.wait_ge(dec_exp, 4)
                link(dve.tensor_tensor(kg, kg, beta[:, 1, :], ALU.mult))
                link(dve.tensor_tensor(kg, kg, rk[:, 1, :], ALU.mult))
                link(dve.tensor_tensor(kd, kd, rk[:, 0, :], ALU.mult))
                link(dve.tensor_scalar(so, rq, float(P) ** -0.5, None, ALU.mult))
                link(dve.tensor_tensor(so2, so, so, ALU.mult))
                link(dve.tensor_scalar(so2, so2, 1.0 / P, None, ALU.mult))
                for t in range(TT):
                    link(dve.tensor_tensor(attnT[:, t], attnT[:, t], over_heads(upper), ALU.mult))
                    link(dve.tensor_tensor(attnT[:, t], attnT[:, t], along(rk[:, t, :], P), ALU.mult))
                    link(dve.tensor_tensor(Achunk[:, t], attnT[:, t], over_heads(strict), ALU.mult))
                for t in range(TT):
                    dve.wait_ge(row_ps, 3 + t)
                    dve.tensor_tensor(Achunk[:, t], heads(ps[6 + t]), Achunk[:, t], ALU.mult).then_inc(brow_taken, 1)
                for n, (dst, scale) in enumerate(((KN[:, 0], kd), (KN[:, 1], kg), (Vn[:, 0], beta[:, 0, :]),
                                                  (Vn[:, 1], beta[:, 1, :]))):
                    dve.wait_ge(nat_ps, n + 1)
                    dve.tensor_tensor(dst, heads(ps[NAT[n]]), along(scale, P), ALU.mult).then_inc(nat_ready, 1)
                dve.wait_ge(brow_taken, 2)
                dve.wait_ge(lev_in, 16)

                def off(n, t, b):
                    return dve.tensor_tensor(Aoff[t][:, PAIR[b]], Achunk[:, t, PAIR[b]], over_heads(lev[:, n], 2),
                                             ALU.mult)

                for t in range(TT):
                    dve.wait_ge(kk_ps, 2 * t + 1)
                    link(dve.tensor_tensor(Achunk[:, t], heads(ps[NAT[2 * t]]), Achunk[:, t], ALU.mult))
                    for b in range(2):
                        link(off(0, t, b))
                        dve.tensor_tensor(Bm[t][:, PAIR[b]], over_heads(ident, 2), Aoff[t][:, PAIR[b]],
                                          ALU.subtract).then_inc(B_ready, 1)
                for t in range(TT):
                    dve.wait_ge(kk_ps, 2 * t + 2)
                    dve.tensor_tensor(attnT[:, t], heads(ps[NAT[2 * t + 1]]), attnT[:, t], ALU.mult).then_inc(kk_taken, 1)
                for t, b in BLOCKS:
                    dve.wait_ge(B_ready, 2 * t + b + 1)
                    off(1, t, b).then_inc(aoff_ready, 1)
                dve.wait_ge(eG_ready, 1)
                dve.tensor_tensor(Q[:, :, P:T], Q[:, :, P:T], eG, ALU.mult).then_inc(qdec_ready, 1)
                for n in range(1, LEVELS):
                    if n < LEVELS - 1:
                        for t, b in BLOCKS:
                            dve.wait_ge(m1_ps, 4 * (n - 1) + 2 * t + b + 1)
                            off(n + 1, t, b).then_inc(aoff_ready, 1)
                    if 2 <= n <= 5:
                        u = U_OUT0 + n // 4
                        split_lo(dve, u, u % NS, halves=(n % 2,))
                    for t, b in BLOCKS:
                        j = 4 * (n - 1) + 2 * t + b
                        dve.wait_ge(upd_ps, j + 1)
                        if n < LEVELS - 1:
                            dve.wait_ge(T_ready, j + 1)
                            dve.tensor_tensor(Tm[t][:, PAIR[b]], Tm[t][:, PAIR[b]], heads(ps[4 + 2 * t + b])[:, PAIR[0]],
                                              ALU.subtract).then_inc(T_ready, 1)
                        dve.wait_ge(B_ready, j + 1)
                        dve.tensor_tensor(Bm[t][:, PAIR[b]], Bm[t][:, PAIR[b]], heads(ps[4 + 2 * t + b])[:, PAIR[1]],
                                          ALU.subtract).then_inc(B_ready, 1)
                dve.wait_ge(u_ps, 2)
                link(dve.tensor_copy(Vn[:, 1], heads(ps[1])))
                dve.wait_ge(ws_ps, 1)
                dve.tensor_tensor(Vn[:, 1], Vn[:, 1], heads(ps[5]), ALU.subtract).then_inc(vnew_ready, 1)
                dve.wait_ge(proj_taken, 14)
                for t in range(TT):
                    dve.wait_ge(o_ssq, t + 1)
                    link(dve.tensor_tensor(om[:, t, :], ps[7][:, t * H:t * H + H], so2[:, t, :], ALU.mult))
                    dve.tensor_scalar(om[:, t, :], om[:, t, :], EPS, None, ALU.add).then_inc(o_ms, 1)
                    x = Q[:, :, t * P:t * P + P]
                    link(dve.scalar_tensor_tensor(x, heads(O[t]), onorm, zs[:, :, t * P:t * P + P], ALU.mult, ALU.mult))
                    dve.wait_ge(o_rt, t + 1)
                    link(dve.reciprocal(orr[:, t, :], om[:, t, :]))
                    link(dve.tensor_tensor(orr[:, t, :], orr[:, t, :], so[:, t, :], ALU.mult))
                    row(t, orr[:, t, :], ident)
                for t in range(TT):
                    dve.wait_ge(row_ps, 5 + t)
                    x = Q[:, :, t * P:t * P + P]
                    dve.tensor_tensor(x, x, heads(ps[t]), ALU.mult).then_inc(mix_ready, 1)
                for n, x in enumerate((Q, ysc)):
                    dve.wait_ge(mix_hi, n + 1)
                    dve.tensor_tensor(hTlo[:, 4 * n:4 * n + 4, :], x, hThi[:, 4 * n:4 * n + 4, :].bitcast(F32),
                                      ALU.subtract).then_inc(mix_lo, 1)
                lo_u(dve, U_FFN)
                dve.wait_ge(x_again, 16)
                for n in range(4):
                    if n == 2:
                        lo_u(dve, U_FFN + 1)
                    h, t = divmod(n, 2)
                    dve.wait_ge((out_ps, unit_used)[t], (h + 1, U_OUT0 + h + 1)[t])
                    x = xres[:, t, h * GW:h * GW + GW]
                    dve.tensor_tensor(x, x, ps[n][:, :], ALU.add).then_inc(out_added, 1)

            @block.tensor
            def _(pe):
                pe.wait_ge(cst_in, 16)
                pe_norm(pe, 0)
                pe.wait_ge(hT_ready, 4)
                pe.wait_ge(wab_lo, 1)
                wh, wl = band(wabhi, KD, 2 * H), band(wablo, KD, 2 * H)
                for k in range(KD):
                    ins = product(pe, ps[1][0:2 * H, 0:T], wh[:, k], wl[:, k], hThi[:, k, :], hTlo[:, k, :],
                                  k == 0, k == KD - 1)
                ins.then_inc(ab_done, 1)

                def project(n):
                    u = n
                    if n >= 2:
                        pe.wait_ge(proj_taken, 2 * (n - 1))
                    wh, wl = band(whi[u % NS], KD, GW), band(wlo[u % NS], KD, GW)
                    pe.wait_ge(lo_ready, 2 * u + 2)
                    for c in range(H):
                        ch = slice(c * P, c * P + P)
                        to = pairs(PROJ[BANKS[n]][c // 2])[:, c % 2, :]
                        for k in range(KD):
                            ins = product(pe, to, wh[:, k, ch], wl[:, k, ch], hThi[:, k, :], hTlo[:, k, :],
                                          k == 0, k == KD - 1)
                    ins.then_inc(unit_used, 1)

                def rows(n0, bank):
                    for n in range(TT):
                        pe.wait_ge(row_ready, n0 + n + 1)
                        pe.matmul(ps[bank + n][:, :], ones, rowbuf[n].rearrange("p h i -> p (h i)"), start=True,
                                  stop=True).then_inc(row_ps, 1)

                project(0)
                pe.wait_ge(ab_rows, 1)
                for t in range(TT):
                    ins = pe.transpose(ps[0][:, t * 2 * H:(t + 1) * 2 * H], ab_chan[:, t * P:t * P + P],
                                       ident[0:2 * H, 0:2 * H])
                ins.then_inc(ab_done, 1)
                project(1)
                pe.wait_ge(g_ready, 1)
                for t in range(TT):
                    ins = pe.matmul(ps[0][:, 32 + t * H:32 + t * H + H], upper, gdec[:, t, :], start=True, stop=True)
                ins.then_inc(gc_ps, 1)
                for n in range(2, 5):
                    project(n)
                    if n == 3:
                        rows(0, 2)
                for n in range(2):
                    pe.wait_ge(l2_sq, n + 1)
                    for t in range(TT):
                        for h in range(H):
                            at = 64 + (n * TT + t) * H + h
                            ins = pe.matmul(ps[0][:, at:at + 1], sq[n][:, h, t * P:t * P + P], ones[:, 0:1],
                                            start=True, stop=True)
                ins.then_inc(l2_ps, 1)
                project(5)
                pe.wait_ge(proj_taken, 10)
                pe.wait_ge(silu_done, 3)
                for n in range(4):
                    if n >= 2:
                        pe.wait_ge((diff_ready, eG_ready)[n - 2], (2, 1)[n - 2])
                    t = n % 2
                    for h in range(H):
                        ins = pe.transpose(heads(ps[NAT[n]])[:, h, :], (K, V)[n // 2][:, h, t * P:t * P + P], ident)
                    ins.then_inc(nat_ps, 1)
                pe.wait_ge(proj_taken, 12)
                rows(2, 6)
                pe.wait_ge(l2_ms, 1)
                project(6)
                for n in range(4):
                    pe.wait_ge(nat_ready, n + 1)
                    t = n // 2
                    tok = slice(t * P, t * P + P)
                    for h in range(H):
                        ins = pe.matmul(heads(ps[NAT[n]])[:, h, :], K[:, h, tok], (K, Q)[n % 2][:, h, tok],
                                        start=True, stop=True)
                    ins.then_inc(kk_ps, 1)
                pe.wait_ge(kk_taken, 2)
                for t, b in BLOCKS:
                    pe.wait_ge(B_ready, 2 * t + b + 1)
                    for h in range(2):
                        ins = pe.transpose(heads(ps[4 + 2 * t + b])[:, h, :], Bm[t][:, 2 * b + h], ident)
                    ins.then_inc(tri_init, 1)
                pe.wait_ge(proj_taken, 14)
                for n in range(1, LEVELS):
                    for t, b in BLOCKS:
                        j = 4 * (n - 1) + 2 * t + b
                        pe.wait_ge(aoff_ready, j + 1)
                        pe.wait_ge(T_ready, j + 1)
                        for h in range(2):
                            ins = pe.matmul(heads(ps[2 * t + b])[:, h, :], Aoff[t][:, 2 * b + h], Tm[t][:, 2 * b + h],
                                            start=True, stop=True)
                        ins.then_inc(m1_ps, 1)
                    for t, b in BLOCKS:
                        j = 4 * (n - 1) + 2 * t + b
                        pe.wait_ge(m1_ready, j + 1)
                        pe.wait_ge(B_ready, j + 1)
                        if n < LEVELS - 1:
                            for h in range(2):
                                pe.matmul(heads(ps[4 + 2 * t + b])[:, h, :], Bm[t][:, 2 * b + h], M1[t][:, 2 * b + h],
                                          start=True, stop=True)
                        for h in range(2):
                            ins = pe.matmul(heads(ps[4 + 2 * t + b])[:, 2 + h, :], M1[t][:, 2 * b + h], Bm[t][:, 2 * b + h],
                                            start=True, stop=True)
                        ins.then_inc(upd_ps, 1)
                for t in range(TT):
                    pe.wait_ge(B_ready, 4 * (LEVELS - 1) + 2 * t + 2)
                    for h in range(H):
                        ins = pe.matmul(heads(ps[t])[:, h, :], Bm[t][:, h], Vn[:, t, h], start=True, stop=True)
                    ins.then_inc(u_ps, 1)
                for h in range(H):
                    ins = pe.matmul(heads(ps[2])[:, h, :], KN[:, 1, h], Bm[1][:, h], start=True, stop=True)
                ins.then_inc(u_ps, 1)
                pe.wait_ge(u_ready, 1)
                for h in range(H):
                    ins = pe.matmul(heads(ps[3])[:, h, :], KN[:, 0, h], Vn[:, 0, h], start=True, stop=True)
                ins.then_inc(s1_ps, 1)
                for h in range(H):
                    ins = pe.matmul(heads(O[0])[:, h, :], Vn[:, 0, h], attnT[:, 0, h], start=True, stop=True)
                ins.then_inc(o_ps, 1)
                pe.wait_ge(u_ready, 2)
                pe.wait_ge(s1_ready, 1)
                for h in range(H):
                    ins = pe.matmul(heads(ps[5])[:, h, :], wT[:, h], S1[:, h], start=True, stop=True)
                ins.then_inc(ws_ps, 1)
                pe.wait_ge(vnew_ready, 1)
                pe.wait_ge(qdec_ready, 1)
                for h in range(H):
                    pe.matmul(heads(O[1])[:, h, :], S1[:, h], Q[:, h, P:T], start=True, stop=False)
                    ins = pe.matmul(heads(O[1])[:, h, :], Vn[:, 1, h], attnT[:, 1, h], start=False, stop=True)
                ins.then_inc(o_ps, 1)
                for t in range(TT):
                    pe.wait_ge(o_sq, t + 1)
                    for h in range(H):
                        ins = pe.matmul(ps[7][:, t * H + h:t * H + h + 1], osq[:, t, h * P:h * P + P], ones[:, 0:1],
                                        start=True, stop=True)
                    ins.then_inc(o_ssq, 1)
                rows(4, 0)
                pe.wait_ge(mix_lo, 2)
                for h in range(2):
                    u = U_OUT0 + h
                    for t in range(TT):
                        ins = tokens_by_columns(pe, u, ps[2 * h + t][:, :], t)
                        ins.then_inc((out_ps, unit_used)[t], 1)
        with nc.Block() as block:
            u0, n0 = U_FFN, U_FFN // NS

            def unit_of(i):
                return u0 + 3 * i - 1, u0 + 3 * i, u0 + 3 * i + 1

            def down_unit(i):
                return u0 + 3 * NF - 1 if isinstance(i, int) and i == NF - 1 else u0 + 3 * i + 4

            gated_hi, gated_lo = (x[:, :, :, :].rearrange("p t c i -> p t (c i)") for x in (aThi, aTlo))
            Y4 = ps[4:8]

            @block.sync
            def _(sp):
                swiglu_loads(sp, u0, ffn_col(w1f), ffn_col(w3f), ffn_down)
                for u in range(U_IN1, U_IN1 + 3):
                    load(sp, u, u % NS, *odd_unit(u))

            @block.scalar
            def _(act):
                act_norm(act, 1, (out_added, 4))
                act_silu(act, TT, u0, 0)

                def round_gated(i):
                    act.wait_ge(unit_used, u0 + 3 * i + 2)
                    for b in range(2):
                        act.wait_ge(a_ready, 2 * i + b + 1)
                        act.copy(gated_hi[:, b, :], actf[:, b, :]).then_inc(aThi_ready, 1)

                with act.Fori(1, NF) as i:
                    w1, w3, w2 = unit_of(i)
                    split_hi(act, w1, 2, n0 + i - 1)
                    split_hi(act, w3, 0, n0 + i)
                    round_gated(i - 1)
                    split_hi(act, w2, 1, n0 + i)
                    act_silu(act, TT, w1, 2 * i)
                split_hi(act, u0 + 3 * NF - 1, 2, n0 + NF - 1)
                round_gated(NF - 1)
                hi_u(act, U_IN1, UNIT // 2)
                hi_u(act, U_IN1 + 1)
                act.wait_ge(xn_ready, 4)
                act.dma_start(gain, a["od_norm1"].to_broadcast([P, D])).then_inc(gain_in, 16)
                act_square(act, 0, (y_added, 4 * NF - 2))

            @block.vector
            def _(dve):
                link = linker(dve)
                dve_norm(dve, 1, link)

                def add_y(i, part):
                    for n in part:
                        t, h = divmod(n, 2)
                        if n < 3:
                            dve.wait_ge(y_done, 3 * i + n + 1)
                        else:
                            dve.wait_ge(unit_used, down_unit(i) + 1)
                        if not (isinstance(i, int) and i == 0):
                            dve.wait_ge(y_added, 4 * i + n - 3)
                        x = xres[:, t, h * GW:h * GW + GW]
                        dve.tensor_tensor(x, x, Y4[n][:, :], ALU.add).then_inc(y_added, 1)

                def gate(i, w3):
                    if not (isinstance(i, int) and i == 0):
                        dve.wait_ge(aTlo_ready, 2 * i)
                    dve_gate(dve, TT, w3, 2 * i)

                def split_gated(i):
                    for b in range(2):
                        dve.wait_ge(aThi_ready, 2 * i + b + 1)
                        dve.tensor_tensor(gated_lo[:, b, :], actf[:, b, :], gated_hi[:, b, :].bitcast(F32),
                                          ALU.subtract).then_inc(aTlo_ready, 1)

                gate(0, u0 + 1)
                split_lo(dve, u0 + 2, 2)

                def step(i, last):
                    w1, w3, w2 = unit_of(i)
                    split_lo(dve, w3, 0)
                    split_gated(i - 1)
                    split_lo(dve, w2, 1)
                    split_lo(dve, w1 + 3, 2)
                    gate(i, w3)
                    if last:
                        split_gated(i)
                    add_y(i - 1, range(4))

                step(1, False)
                with dve.Fori(2, NF - 1) as i:
                    step(i, False)
                step(NF - 1, True)
                lo_u(dve, U_IN1, UNIT // 2)
                add_y(NF - 1, (0,))
                split_lo(dve, U_IN1 + 1, (U_IN1 + 1) % NS, halves=(0,))
                add_y(NF - 1, (1,))
                split_lo(dve, U_IN1 + 1, (U_IN1 + 1) % NS, halves=(1,))
                add_y(NF - 1, (2, 3))

            @block.tensor
            def _(pe):
                pe_norm(pe, 1)

                def up(u, s, to, fresh=None):
                    wh, wl = band(whi[s], KD, GW), band(wlo[s], KD, GW)
                    for c in range(FC):
                        ch = slice(c * P, c * P + P)
                        for k in range(KD):
                            if c == 0 and fresh is not None and k % 2 == 0:
                                pe.wait_ge(hT_ready, 4 * fresh + k // 2 + 1)
                            if c == 0 and k % 4 == 0:
                                pe.wait_ge(lo_ready, 2 * u + k // 4 + 1)
                            ins = product(pe, pairs(to[c // 2])[:, c % 2, :], wh[:, k, ch], wl[:, k, ch],
                                          hThi[:, k, :], hTlo[:, k, :], k == 0, k == KD - 1)
                    ins.then_inc(unit_used, 1)

                def down_step(i, s):
                    gh, gl = (x.rearrange("p b (c t) -> p (b c) t", c=2) for x in (gated_hi, gated_lo))
                    wh, wl = band(whi[s], FC, D), band(wlo[s], FC, D)
                    pe.wait_ge(aTlo_ready, 2 * i + 2)
                    pe.wait_ge(lo_ready, 2 * down_unit(i) + 2)
                    for n in range(4):
                        t, h = divmod(n, 2)
                        tok, col = slice(t * P, t * P + P), slice(h * GW, h * GW + GW)
                        if not (isinstance(i, int) and i == 0):
                            pe.wait_ge(y_added, 4 * i + n - 3)
                        for c in range(FC):
                            ins = product(pe, Y4[n][:, :], gh[:, c, tok], gl[:, c, tok], wh[:, c, col], wl[:, c, col],
                                          c == 0, c == FC - 1)
                        ins.then_inc(y_done if n < 3 else unit_used, 1)

                up(u0, 0, H1, fresh=1)
                up(u0 + 1, 1, H3)

                def step(i):
                    w1, w3, w2 = unit_of(i)
                    pe.wait_ge(sil_ready, 2 * i)
                    up(w1, 2, H1)
                    pe.wait_ge(a_ready, 2 * i)
                    up(w3, 0, H3)
                    down_step(i - 1, 1)

                step(1)
                with pe.Fori(2, NF) as i:
                    step(i)
                down_step(NF - 1, 2)
        (qkv_ps, qkv_taken, h_sq, h_ms, h_rt, qk_ready, qT_ps, qT_ready, kT_ready, sc_ps, neg_max,
         p_ready, pT_ps, pT_ready, av_ps, es_in, es_exp, ao_ready, aoT_ps, aoT_hi, aoT_lo) = sem(
            "qkv_ps qkv_taken h_sq h_ms h_rt qk_ready qT_ps qT_ready kT_ready sc_ps neg_max "
            "p_ready pT_ps pT_ready av_ps es_in es_exp ao_ready aoT_ps aoT_hi aoT_lo")
        QK = QH + KVH

        def place(h):
            return 2 * (h % 2) + h // 2

        GROUPS = [(QH * HD, 2 * KVH * HD, slice(QH, QK)), (0, GW, slice(0, QH // 2)), (GW, GW, slice(QH // 2, QH))]
        QBANK = [7, 6, 4, 5]

        def heads_of(t, hs):
            return qkv[:, t, hs.start * HD:hs.stop * HD].rearrange("p (h d) -> p h d", d=HD)

        with nc.Block() as block:
            @block.sync
            def _(sp):
                for u in (U_OUT1, U_OUT1 + 1, U_ROUTER):
                    load(sp, u, u % NS, *odd_unit(u))
                first_loads(sp, U_MOE, moe_col(w1m, 0), moe_col(w3m, 0))

            @block.scalar
            def _(act):
                act.dma_start(masks, a["consts"][:, C_MASK:C_ALL].rearrange("p (a i) -> p a i", a=2)).then_inc(mask_in, 16)
                act_norm(act, 2, (y_added, 4 * NF))
                hi_u(act, U_IN1 + 2)

                def take_turned(b):
                    act.wait_ge(qT_ps, b + 2)
                    act.copy(qT[:, 2 * b:2 * b + 2, :], pairs(ps[QBANK[b]])).then_inc(qT_ready, 1)

                for c, (col, n, hs) in enumerate(GROUPS):
                    for t in range(TT):
                        if t == 0:
                            act.wait_ge(qkv_ps, c + 1)
                        else:
                            act.wait_ge(unit_used, U_IN1 + c + 1)
                        act.copy(qkv[:, t, col:col + n], ps[2 * c + t][:, 0:n]).then_inc(qkv_taken, 1)
                    act.wait_ge(qkv_taken, 2 * c + 2)
                    for t in range(TT):
                        act.activation(hsq[:, t, hs], heads_of(t, hs), ACT.Square).then_inc(h_sq, 1)
                    if c == 2:
                        take_turned(0)
                        take_turned(1)
                    act.wait_ge(h_ms, c + 1)
                    act.activation(hrs[:, :, hs], hss[:, :, hs], ACT.Sqrt).then_inc(h_rt, 1)
                    if c == 1:
                        hi_u(act, U_OUT1)
                        hi_u(act, U_OUT1 + 1)
                hi_u(act, U_ROUTER, KD * NE)
                take_turned(2)
                take_turned(3)
                for j in range(8):
                    t, g = divmod(j, 4)
                    keys = P * (1 + t)
                    act.wait_ge(neg_max, j + 1)
                    for h in range(4):
                        hh = 4 * g + h
                        at = place(h) * keys
                        x = prob[j % 2][:, at:at + keys]
                        act.activation(x, x, ACT.Exp, bias=nmax[t][:, hh:hh + 1],
                                       accum_out=rsum[t][:, hh:hh + 1]).then_inc(p_ready, 1)
                    if g == 3:
                        act.wait_ge(es_in, t + 1)
                        act.activation(esink[t], esink[t], ACT.Exp).then_inc(es_exp, 1)
                for b in range(4):
                    act.wait_ge(aoT_ps, b + 1)
                    act.copy(hThi[:, 2 * b:2 * b + 2, :], pairs(ps[b])).then_inc(aoT_hi, 1)
                act.dma_start(gain, a["od_norm2"].to_broadcast([P, D])).then_inc(gain_in, 16)
                hi_u(act, U_MOE)
                act_square(act, 0, (out_added, 7))

            @block.vector
            def _(dve):
                link = linker(dve)
                dve_norm(dve, 2, link)
                lo_u(dve, U_IN1 + 2)
                for c, (col, n, hs) in enumerate(GROUPS):
                    if c == 1:
                        dve.wait_ge(qT_ps, 1)
                        dve.tensor_copy(kT, pairs(ps[6])).then_inc(kT_ready, 1)
                    for t in range(TT):
                        dve.wait_ge(h_sq, TT * c + t + 1)
                        dve.tensor_reduce(hss[:, t, hs], hsq[:, t, hs], AX.X, ALU.add).then_inc(dve_step, 1)
                    steps["dve"] += TT
                    dve.wait_ge(dve_step, steps["dve"])
                    dve.tensor_scalar(hss[:, :, hs], hss[:, :, hs], 1.0 / HD, EPS, ALU.mult, ALU.add).then_inc(h_ms, 1)
                    dve.wait_ge(h_rt, c + 1)
                    link(dve.reciprocal(hrs[:, :, hs], hrs[:, :, hs]))
                    for t in range(TT):
                        x = heads_of(t, hs)
                        link(dve.tensor_tensor(x, x, along(hrs[:, t, hs], HD), ALU.mult))
                        if c:
                            dve.tensor_tensor(x, x, over_heads(qnw, QH // 2), ALU.mult).then_inc(qk_ready, 1)
                            continue
                        for m in range(2):
                            dve.tensor_tensor(kdup[:, t, :, m, :], x, over_heads(knw, KVH), ALU.mult).then_inc(qk_ready, 1)
                    if c == 1:
                        lo_u(dve, U_OUT1)
                dve.wait_ge(mask_in, 16)

                def masked(j):
                    t, g = divmod(j, 4)
                    keys = P * (1 + t)
                    if j >= 2:
                        dve.wait_ge(pT_ps, j - 1)
                    dve.wait_ge(sc_ps, j + 1)
                    x = prob[j % 2][:, 0:4 * keys].rearrange("p (h k) -> p h k", h=4)
                    m = masks.rearrange("p a i -> p (a i)")[:, P - P * t:2 * P]
                    for b in range(2):
                        s = ps[2 * (j % 2) + b][:, 0:2 * keys].rearrange("p (h k) -> p h k", h=2)
                        link(dve.scalar_tensor_tensor(x[:, 2 * b:2 * b + 2], s, HD ** -0.5, over_heads(m, 2),
                                                      ALU.mult, ALU.add))
                    hs = slice(4 * g, 4 * g + 4)
                    link(dve.tensor_reduce(smax[t][:, hs].rearrange("p (m b) -> p b m", b=2),
                                           x.rearrange("p (b m) k -> p b m k", b=2), AX.X, ALU.max))
                    link(dve.tensor_tensor(smax[t][:, hs], smax[t][:, hs], sinks[:, hs], ALU.max))
                    dve.tensor_scalar(nmax[t][:, hs], smax[t][:, hs], -1.0, None, ALU.mult).then_inc(neg_max, 1)

                def turned(j):
                    t, g = divmod(j, 4)
                    dve.wait_ge(pT_ps, j + 1)
                    if j >= 2:
                        dve.wait_ge(av_ps, j - 1)
                    for b in range(1 + t):
                        ins = dve.tensor_copy(probT[j % 2][:, 4 * b:4 * b + 4, :],
                                              ps[4 + b][:, :].rearrange("p (c i) -> p c i", c=4))
                    ins.then_inc(pT_ready, 1)

                def outputs(t):
                    dve.wait_ge(p_ready, 16 * (t + 1))
                    dve.wait_ge(es_exp, t + 1)
                    link(dve.tensor_tensor(rsum[t], rsum[t], esink[t], ALU.add))
                    link(dve.reciprocal(rsum[t], rsum[t]))
                    dve.wait_ge(av_ps, 4 * t + 4)
                    for b in range(2):
                        dve.tensor_tensor(ao(t, b), ps[6 + b][:, :].rearrange("p (h d) -> p h d", d=HD),
                                          along(rsum[t][:, 8 * b:8 * b + 8], HD), ALU.mult).then_inc(ao_ready, 1)

                def ao(t, b):
                    return qkv[:, t, b * GW:b * GW + GW].rearrange("p (h d) -> p h d", d=HD)

                for t in range(TT):
                    for g in range(4):
                        masked(4 * t + g)
                        if g == 3:
                            dve.tensor_tensor(esink[t], sinks, smax[t], ALU.subtract).then_inc(es_in, 1)
                        j = 4 * t + g
                        if j in (1, 2):
                            u = U_OUT1 + 1
                            split_lo(dve, u, u % NS, halves=(j - 1,))
                        if j == 3:
                            lo_u(dve, U_ROUTER, KD * NE)
                        if j:
                            turned(j - 1)
                        if j == 4:
                            outputs(0)
                turned(7)
                outputs(1)
                for b in range(4):
                    dve.wait_ge(aoT_hi, b + 1)
                    dve.tensor_tensor(hTlo[:, 2 * b:2 * b + 2, :], pairs(ps[b]),
                                      hThi[:, 2 * b:2 * b + 2, :].bitcast(F32), ALU.subtract).then_inc(aoT_lo, 1)
                for n in range(4):
                    if n == 2:
                        lo_u(dve, U_MOE)
                    h, t = divmod(n, 2)
                    dve.wait_ge((out_ps, unit_used)[t], (3 + h, U_OUT1 + h + 1)[t])
                    x = xres[:, t, h * GW:h * GW + GW]
                    dve.tensor_tensor(x, x, ps[4 + n][:, :], ALU.add).then_inc(out_added, 1)

            @block.tensor
            def _(pe):
                pe_norm(pe, 2)
                def turn_q(b):
                    for k in (2 * b, 2 * b + 1):
                        for t in range(TT):
                            ins = pe.transpose(pairs(ps[QBANK[b]])[:, k % 2, t * P:t * P + P],
                                               qkv[:, t, k * P:k * P + P], ident)
                    ins.then_inc(qT_ps, 1)

                for c, (col, n, hs) in enumerate(GROUPS):
                    for t in range(TT):
                        ins = tokens_by_columns(pe, U_IN1 + c, ps[2 * c + t][:, 0:n], t, n=n, fresh=None if c else 2)
                        ins.then_inc((qkv_ps, unit_used)[t], 1)
                    if c == 1:
                        pe.wait_ge(qk_ready, 4)
                        for g in range(KVH):
                            for t in range(TT):
                                ins = pe.transpose(pairs(ps[6])[:, g, t * P:t * P + P],
                                                   kdup[:, t, g].rearrange("p n d -> p (n d)"), ident)
                        ins.then_inc(qT_ps, 1)
                pe.wait_ge(kT_ready, 1)
                pe.wait_ge(qk_ready, 6)
                turn_q(0)
                turn_q(1)
                pe.wait_ge(qT_ready, 2)

                def scores(j):
                    t, g = divmod(j, 4)
                    if j >= 2:
                        pe.wait_ge(neg_max, j - 1)
                    for h in range(4):
                        hh = 4 * g + h
                        rows = slice(HD * (hh % 2), HD * (hh % 2) + HD)
                        keys = P * (1 + t)
                        at = (h // 2) * keys
                        ins = pe.matmul(ps[2 * (j % 2) + h % 2][:, at:at + keys], qT[rows, hh // 2, t * P:t * P + P],
                                        kT[rows, hh // GRP, 0:keys], start=True, stop=True)
                    ins.then_inc(sc_ps, 1)

                def turn(j):
                    t, g = divmod(j, 4)
                    pe.wait_ge(p_ready, 4 * j + 4)
                    if j:
                        pe.wait_ge(pT_ready, j)
                    for c in range(4 * (1 + t)):
                        ins = pe.transpose(ps[4 + c // 4][:, (c % 4) * P:(c % 4) * P + P],
                                           prob[j % 2][:, c * P:c * P + P], ident)
                    ins.then_inc(pT_ps, 1)

                def values(j):
                    t, g = divmod(j, 4)
                    pe.wait_ge(pT_ready, j + 1)
                    if t and g == 0:
                        pe.wait_ge(ao_ready, 2)
                    for h in range(4):
                        hh = 4 * g + h
                        to = ps[6 + hh // 8][:, (hh % 8) * HD:(hh % 8) * HD + HD]
                        for kb in range(1 + t):
                            v = qkv[:, kb, (QK + hh // GRP) * HD:(QK + hh // GRP + 1) * HD]
                            ins = pe.matmul(to, probT[j % 2][:, place(h) * (1 + t) + kb, :], v, start=kb == 0, stop=kb == t)
                    ins.then_inc(av_ps, 1)

                scores(0)
                scores(1)
                pe.wait_ge(qk_ready, 8)
                turn_q(2)
                turn_q(3)
                pe.wait_ge(qT_ready, 4)
                for j in range(8):
                    turn(j)
                    if j + 2 < 8:
                        scores(j + 2)
                    values(j)
                pe.wait_ge(ao_ready, 4)
                for k in range(KD):
                    for t in range(TT):
                        ins = pe.transpose(pairs(ps[k // 2])[:, k % 2, t * P:t * P + P], qkv[:, t, k * P:k * P + P], ident)
                    if k % 2:
                        ins.then_inc(aoT_ps, 1)
                pe.wait_ge(aoT_lo, 4)
                for h in range(2):
                    for t in range(TT):
                        ins = tokens_by_columns(pe, U_OUT1 + h, ps[4 + 2 * h + t][:, :], t)
                        ins.then_inc((out_ps, unit_used)[t], 1)
        (rt_in, rt_exp, rank_in, rank_ps, flag_ready, sel_ready, xg_ps, xghi_ready,
         xglo_ready, PT_ps, PT_ready, yhi_ready, ylo_ready, sc_done, sc_added, out_sent, rcol_ready,
         gcol_ready) = sem(
            "rt_in rt_exp rank_in rank_ps flag_ready sel_ready xg_ps xghi_ready "
            "xglo_ready PT_ps PT_ready yhi_ready ylo_ready sc_done sc_added out_sent rcol_ready gcol_ready")
        GATHER = [H1[1], H3[1]]
        SCATTER = [H1[1], H3[1], H1[1], H3[1]]
        G0 = 2 * NF

        second = sm(468, TT)
        by_expert = Psel[0:NE].rearrange("p t i -> p (t i)")
        rt_rows, rt_ps = sem("rt_rows rt_ps")

        def slots_of(t):
            return Psel[:, t, :]

        with nc.Block() as block:
            out_t = out[0].rearrange("(t p) d -> p t d", p=P)

            def units(q, e, i):
                u0 = U_MOE + U_PASS * q + 3 * NF * e
                return u0 + 3 * i - 1, u0 + 3 * i, u0 + 3 * i + 1

            def down_unit(q, e):
                return U_MOE + U_PASS * (q + 1) - 1 if isinstance(e, int) and e == NE - 1 else units(q, e, NF)[2]

            def uses(q, e):
                return (U_MOE + U_PASS * q) // NS + NF * e

            def tiles(q, e, i):
                return G0 + NF * NE * q + NF * e + i

            @block.sync
            def _(sp):
                def moe_loads(q):
                    def step(e, i, w1):
                        _, u, _ = units(q, e, i)
                        load(sp, u, 0, band(raw[0], KD, GW), moe_col(w3m, e)(i))
                        load(sp, u + 1, 1, band(raw[1], FC, D), moe_down(e)(i - 1))
                        if w1 is not None:
                            load(sp, u + 2, 2, band(raw[2], KD, GW), w1)

                    def expert(e, last):
                        with sp.Fori(1, NF - 1) as i:
                            step(e, i, moe_col(w1m, e)(i + 1))
                        if last:
                            step(e, NF - 1, None)
                            return
                        step(e, NF - 1, moe_col(w1m, e + 1)(0))
                        u = units(q, e, NF)[1]
                        load(sp, u, 0, band(raw[0], KD, GW), moe_col(w3m, e + 1)(0))
                        load(sp, u + 1, 1, band(raw[1], FC, D), moe_down(e)(NF - 1))
                        load(sp, u + 2, 2, band(raw[2], KD, GW), moe_col(w1m, e + 1)(1))

                    with sp.Fori(0, NE - 1) as e:
                        expert(e, False)
                    expert(NE - 1, True)
                    load(sp, U_MOE + U_PASS * (q + 1) - 1, 2, band(raw[2], FC, D), moe_down(NE - 1)(NF - 1))

                moe_loads(0)
                sp.wait_ge(sc_added, 4 * NE)
                sp.dma_start(out_t, xres[:, :, :]).then_inc(out_sent, 16)
                sp.wait_ge(out_sent, 16)
                sp.wait_ge(flag_ready, 1)
                more = sp.value_load(flag[0:1, 0:1], min_val=0, max_val=1)
                with sp.If(more == 1):
                    first_loads(sp, U_MOE + U_PASS, moe_col(w1m, 0), moe_col(w3m, 0))
                    moe_loads(1)
                    sp.wait_ge(sc_added, 8 * NE)
                    sp.dma_start(out_t, xres[:, :, :]).then_inc(out_sent, 16)
                    sp.wait_ge(out_sent, 32)
                sp.nop()

            @block.scalar
            def _(act):
                act_norm(act, 3, (out_added, 8), between=[lambda: hi_u(act, U_MOE + 1)])
                act.wait_ge(rt_in, 1)
                act.activation(second, second, ACT.Exp).then_inc(rt_exp, 1)

                def gathered(n):
                    act.wait_ge(xg_ps, n + 1)
                    for b in range(2):
                        act.copy(xghi[:, 4 * b:4 * b + 4, :], heads(GATHER[b])).then_inc(xghi_ready, 1)

                def expert_out(q, e):
                    act.wait_ge(unit_used, down_unit(q, e) + 1)
                    for h in range(2):
                        act.copy(yhi[:, 4 * h:4 * h + 4, :], heads(Y[h])).then_inc(yhi_ready, 1)

                def step(q, e, i, before_w3=None, before_aT=None, split_w1=True):
                    n0 = uses(q, e)
                    w1, w3, w2 = units(q, e, i)
                    if split_w1:
                        split_hi(act, w1, 2, n0 + i - 1)
                    if before_w3:
                        before_w3()
                    split_hi(act, w3, 0, n0 + i)
                    if before_aT:
                        before_aT()
                    order = [lambda: act_aT(act, tiles(q, e, i - 1)), lambda: split_hi(act, w2, 1, n0 + i)]
                    for work in order if split_w1 else order[::-1]:
                        work()
                    act_silu(act, 1, w1, tiles(q, e, i))

                def next_input(q, e):
                    act.wait_ge(unit_used, units(q, e, NF - 1)[1] + 1)
                    gathered(NE * q + e + 1)

                def expert(q, e):
                    first = isinstance(e, int) and e == 0
                    step(q, e, 1, before_aT=None if first else lambda: expert_out(q, e - 1), split_w1=not first)
                    with act.Fori(2, NF) as i:
                        step(q, e, i)
                    if not (isinstance(e, int) and e == NE - 1):
                        step(q, e, NF, before_w3=lambda: next_input(q, e))

                def moe(q):
                    for n in range(NS) if q else (2,):
                        split_hi(act, U_MOE + U_PASS * q + n, n, uses(q, 0))
                    gathered(NE * q)
                    act_silu(act, 1, U_MOE + U_PASS * q, tiles(q, 0, 0))
                    expert(q, 0)
                    with act.Fori(1, NE - 1) as e:
                        expert(q, e)
                    expert(q, NE - 1)
                    split_hi(act, down_unit(q, NE - 1), 2, uses(q, NE) - 1)
                    act_aT(act, tiles(q, NE, -1))
                    expert_out(q, NE - 1)

                moe(0)
                act.wait_ge(flag_ready, 1)
                more = act.value_load(flag[0:1, 0:1], min_val=0, max_val=1)
                with act.If(more == 1):
                    moe(1)
                act.nop()

            @block.vector
            def _(dve):
                link = linker(dve)
                dve_norm(dve, 3, link)
                split_lo(dve, U_MOE + 1, 1)
                lg, eq, idx, oh1, l2g, oh2, tmp, gate = lgt[0:8]
                it = iota[:, 0:NE]
                dve.wait_ge(unit_used, U_ROUTER + 1)
                dve.tensor_copy(by_expert, ps[4][0:NE, 0:T]).then_inc(rt_rows, 1)
                dve.wait_ge(rt_ps, 1)
                link(dve.tensor_copy(lg, ps[5][:, 0:TT * NE].rearrange("p (t n) -> p t n", t=TT)))
                v = [sm(472 + 2 * n, TT) for n in range(4)]

                def best(x, value, index, onehot):
                    link(dve.tensor_reduce(value, x, AX.X, ALU.max))
                    link(dve.tensor_tensor(eq, x, along(value, NE), ALU.is_lt))
                    link(dve.scalar_tensor_tensor(tmp, eq, float(P), over_heads(it, TT), ALU.mult, ALU.add))
                    link(dve.tensor_reduce(index, tmp, AX.X, ALU.min))
                    link(dve.tensor_tensor(onehot, over_heads(it, TT), along(index, NE), ALU.is_equal))

                best(lg, v[0], v[1], oh1)
                link(dve.tensor_scalar(eq, oh1, -1.0, 1.0, ALU.mult, ALU.add))
                link(dve.tensor_tensor(l2g, lg, eq, ALU.mult))
                link(dve.scalar_tensor_tensor(l2g, oh1, -3.0e38, l2g, ALU.mult, ALU.add))
                best(l2g, v[2], v[3], oh2)
                dve.tensor_tensor(second, v[2], v[0], ALU.subtract).then_inc(rt_in, 1)
                chosen = lgt[8]
                link(dve.tensor_tensor(chosen, oh1, oh2, ALU.add))
                dve.tensor_copy(eq, chosen).then_inc(rank_in, 1)
                dve.wait_ge(rt_exp, 1)
                link(dve.tensor_scalar(v[0], second, 1.0, None, ALU.add))
                link(dve.reciprocal(v[0], v[0]))
                link(dve.tensor_tensor(v[1], second, v[0], ALU.mult))
                link(dve.tensor_tensor(gate, oh1, along(v[0], NE), ALU.mult))
                link(dve.tensor_tensor(tmp, oh2, along(v[1], NE), ALU.mult))
                link(dve.memset(gates, 0.0))
                link(dve.tensor_tensor(gates[:, :, 0:NE], gate, tmp, ALU.add))
                dve.wait_ge(rank_ps, 1)
                rank = ps[6][:, 0:TT * NE].rearrange("p (t n) -> p t n", t=TT)
                link(dve.memset(slot_of, -1.0))
                link(dve.scalar_tensor_tensor(tmp, rank, 1.0, chosen, ALU.add, ALU.mult))
                link(dve.tensor_scalar(slot_of[:, :, 0:NE], tmp, -1.0, None, ALU.add))
                link(dve.tensor_reduce(cnt[:, 0:1], ps[6][:, 32:32 + NE], AX.X, ALU.max))
                dve.tensor_scalar(flag[0:1, 0:1], cnt[0:1, 0:1], float(CAP), None, ALU.is_gt).then_inc(flag_ready, 1)

                def select(q, e, n):
                    if not (isinstance(n, int) and n == 0):
                        dve.wait_ge(PT_ps, n)
                        dve.wait_ge(sel_ready, 2 * n)
                    link2(dve.tensor_copy(rcol, slot_of[:, :, bass.ds(e, 1)].rearrange("p t n -> p (t n)")), n)
                    for t in range(TT):
                        dve.tensor_scalar(slots_of(t), iota, float(CAP * q), rcol[:, t:t + 1], ALU.add,
                                          ALU.is_equal).then_inc(sel_ready, 1)

                def link2(ins, n):
                    ins.then_inc(rcol_ready, 1)
                    dve.wait_ge(rcol_ready, n + 1)

                def gathered(n):
                    for b in range(2):
                        dve.wait_ge(xghi_ready, 2 * n + b + 1)
                        dve.tensor_tensor(xglo[:, 4 * b:4 * b + 4, :], heads(GATHER[b]),
                                          xghi[:, 4 * b:4 * b + 4, :].bitcast(F32), ALU.subtract).then_inc(xglo_ready, 1)

                def turned(n):
                    dve.wait_ge(PT_ps, n + 1)
                    dve.tensor_copy(PT[:, :, :], TP[1][:, 0:TT * P].rearrange("p (t i) -> p t i", t=TT)).then_inc(PT_ready, 1)

                def expert_out(n):
                    for h in range(2):
                        dve.wait_ge(yhi_ready, 2 * n + h + 1)
                        dve.tensor_tensor(ylo[:, 4 * h:4 * h + 4, :], heads(Y[h]),
                                          yhi[:, 4 * h:4 * h + 4, :].bitcast(F32), ALU.subtract).then_inc(ylo_ready, 1)

                def scattered(e, n, part):
                    if part[0] == 0:
                        dve.tensor_copy(gcol, gates[:, :, bass.ds(e, 1)].rearrange("p t n -> p (t n)")).then_inc(gcol_ready, 1)
                        dve.wait_ge(gcol_ready, n + 1)
                    for j in part:
                        t, h = divmod(j, 2)
                        dve.wait_ge(sc_done, 4 * n + j + 1)
                        x = xres[:, t, h * GW:h * GW + GW]
                        dve.scalar_tensor_tensor(x, SCATTER[j][:, :], gcol[:, t:t + 1], x, ALU.mult,
                                                 ALU.add).then_inc(sc_added, 1)
                    if part[-1] == 3:
                        dve.wait_ge(sc_added, 4 * n + 4)

                def step(q, e, i, split_w3=True, first=None, scat=None, after_gate=None):
                    w1, w3, w2 = units(q, e, i)
                    if split_w3:
                        split_lo(dve, w3, 0)
                    if first:
                        first()
                    order = [lambda: dve_aT(dve, tiles(q, e, i - 1)), lambda: split_lo(dve, w2, 1)]
                    for work in order if split_w3 else order[::-1]:
                        work()
                    split_lo(dve, w2 + 1, 2)
                    if scat:
                        scat((0, 1))
                    dve_gate(dve, 1, w3, tiles(q, e, i))
                    if scat:
                        scat((2, 3))
                    if after_gate:
                        after_gate()

                def expert(q, e):
                    n = NE * q + e
                    first, last = (isinstance(e, int) and e == x for x in (0, NE - 1))

                    def slots():
                        turned(n)
                        if not last:
                            select(q, e + 1, n + 1)

                    step(q, e, 1, split_w3=not first, first=None if first else lambda: expert_out(n - 1),
                         scat=None if first else lambda part: scattered(e - 1, n - 1, part), after_gate=slots)
                    with dve.Fori(2, NF - 1) as i:
                        step(q, e, i)
                    step(q, e, NF - 1, after_gate=None if last else lambda: gathered(n + 1))
                    if not last:
                        step(q, e, NF)

                def moe(q):
                    n0 = NE * q
                    if q:
                        dve.wait_ge(out_sent, 16)
                    select(q, 0, n0)
                    for n in range(NS) if q else (2,):
                        split_lo(dve, U_MOE + U_PASS * q + n, n)
                    gathered(n0)
                    split_lo(dve, U_MOE + U_PASS * q + NS, 0)
                    dve_gate(dve, 1, U_MOE + U_PASS * q + 1, tiles(q, 0, 0))
                    expert(q, 0)
                    with dve.Fori(1, NE - 1) as e:
                        expert(q, e)
                    expert(q, NE - 1)
                    dve_aT(dve, tiles(q, NE, -1))
                    expert_out(n0 + NE - 1)
                    scattered(NE - 1, n0 + NE - 1, (0, 1, 2, 3))

                moe(0)
                dve.wait_ge(flag_ready, 1)
                more = dve.value_load(flag[0:1, 0:1], min_val=0, max_val=1)
                with dve.If(more == 1):
                    moe(1)
                dve.nop()

            @block.tensor
            def _(pe):
                pe_norm(pe, 3)
                s = U_ROUTER % NS
                wh, wl = band(whi[s], KD, NE), band(wlo[s], KD, NE)
                pe.wait_ge(lo_ready, 2 * U_ROUTER + 2)
                for k in range(KD):
                    if k % 2 == 0:
                        pe.wait_ge(hT_ready, 12 + k // 2 + 1)
                    ins = product(pe, ps[4][0:NE, 0:T], wh[:, k], wl[:, k], hThi[:, k, :], hTlo[:, k, :],
                                  k == 0, k == KD - 1)
                ins.then_inc(unit_used, 1)
                pe.wait_ge(rt_rows, 1)
                for t in range(TT):
                    ins = pe.transpose(ps[5][:, t * NE:t * NE + NE], by_expert[:, t * P:t * P + P], ident[0:NE, 0:NE])
                ins.then_inc(rt_ps, 1)
                pe.wait_ge(rank_in, 1)
                chosen = lgt[8]
                pe.matmul(ps[6][:, 0:NE], strict, chosen[:, 0, :], start=True, stop=True)
                pe.matmul(ps[6][:, NE:2 * NE], strict, chosen[:, 1, :], start=True, stop=False)
                pe.matmul(ps[6][:, NE:2 * NE], ones, chosen[:, 0, :], start=False, stop=True)
                for t in range(TT):
                    ins = pe.matmul(ps[6][:, 32:32 + NE], ones, chosen[:, t, :], start=t == 0, stop=t == 1)
                ins.then_inc(rank_ps, 1)

                def gather(n):
                    pe.wait_ge(sel_ready, 2 * n + 2)
                    for k in range(KD):
                        for t in range(TT):
                            ins = pe.matmul(heads(GATHER[k // 4])[:, k % 4, :], xn[:, t, k * P:k * P + P],
                                            slots_of(t), start=t == 0, stop=t == 1)
                    ins.then_inc(xg_ps, 1)

                def turn_slots(n):
                    for t in range(TT):
                        ins = pe.transpose(TP[1][:, t * P:t * P + P], slots_of(t), ident)
                    ins.then_inc(PT_ps, 1)

                def down_product(g, u, s, first, last):
                    pe.wait_ge(aTlo_ready, g + 1)
                    pe.wait_ge(lo_ready, 2 * u + 2)
                    for h in range(2):
                        ins = down(pe, Y[h][:, :], s, h, first, last)
                    ins.then_inc(unit_used, 1)

                def scatter(n, part):
                    if part[0] == 0:
                        pe.wait_ge(ylo_ready, 2 * n + 2)
                        pe.wait_ge(PT_ready, n + 1)
                    for j in part:
                        t, h = divmod(j, 2)
                        if j >= 2:
                            pe.wait_ge(sc_added, 4 * n + j - 1)
                        to = SCATTER[j][:, :]
                        pe.matmul(to, PT[:, t, :], yhi[:, 4 * h:4 * h + 4, :], start=True, stop=False)
                        pe.matmul(to, PT[:, t, :], ylo[:, 4 * h:4 * h + 4, :], start=False, stop=True).then_inc(sc_done, 1)

                def step(q, e, i, scat=None, gath=None, start=False, stop=False, turn_last=False):
                    w1, w3, w2 = units(q, e, i)
                    pe.wait_ge(sil_ready, tiles(q, e, i))
                    pe_up(pe, w1, 2, H1[0])
                    if turn_last:
                        pe_turn(pe, tiles(q, e, i - 1))
                    if scat:
                        scat((0, 1))
                    pe_up(pe, w3, 0, H3[0])
                    if gath:
                        gath()
                    down_product(tiles(q, e, i - 1), w2, 1, start, stop)
                    if scat:
                        scat((2, 3))
                    pe_turn(pe, tiles(q, e, i))

                def expert(q, e):
                    n = NE * q + e
                    first, last = (isinstance(e, int) and e == x for x in (0, NE - 1))
                    step(q, e, 1, scat=None if first else lambda part: scatter(n - 1, part), start=True,
                         turn_last=first)
                    turn_slots(n)
                    step(q, e, 2, gath=None if last else lambda: gather(n + 1))
                    with pe.Fori(3, NF) as i:
                        step(q, e, i)
                    if not last:
                        pe.wait_ge(xglo_ready, 2 * n + 4)
                        step(q, e, NF, stop=True)

                def moe(q):
                    n0 = NE * q
                    u = U_MOE + U_PASS * q
                    gather(n0)
                    pe.wait_ge(xglo_ready, 2 * n0 + 2)
                    pe_up(pe, u, 0, H1[0])
                    pe_up(pe, u + 1, 1, H3[0])
                    expert(q, 0)
                    with pe.Fori(1, NE - 1) as e:
                        expert(q, e)
                    expert(q, NE - 1)
                    down_product(tiles(q, NE, -1), down_unit(q, NE - 1), 2, False, True)
                    scatter(n0 + NE - 1, (0, 1, 2, 3))

                moe(0)
                pe.wait_ge(flag_ready, 1)
                more = pe.value_load(flag[0:1, 0:1], min_val=0, max_val=1)
                with pe.If(more == 1):
                    moe(1)
                pe.nop()


_INS = ["x", "ev_norm1", "ev_w_in", "ev_w_out", "ev_norm2", "ev_ffn_w1", "ev_ffn_w3", "ev_ffn_w2",
        "od_norm1", "od_w_in", "od_w_out", "od_norm2", "od_router", "od_moe_w1", "od_moe_w3", "od_moe_w2"]


def layout(inputs):
    arrays = {n: np.ascontiguousarray(inputs[n]) for n in _INS}
    row = lambda v: np.broadcast_to(np.asarray(v).reshape(1, -1), (P, np.asarray(v).size))
    arrays["params"] = np.ascontiguousarray(np.concatenate([
        row(inputs["ev_a_log"]), row(inputs["ev_dt_bias"]), np.asarray(inputs["ev_o_norm"]).reshape(P, 1),
        np.zeros((P, 3), np.float32),
        np.asarray(inputs["ev_conv_qkv"])[0].reshape(4, 3 * H, P).transpose(2, 1, 0).reshape(P, 12 * H),
        np.asarray(inputs["ev_conv_sc"])[0].reshape(3, H, P).transpose(2, 1, 0).reshape(P, 3 * H),
        row(inputs["od_q_norm"]), row(inputs["od_k_norm"]), row(inputs["od_sinks"])], axis=1))
    arrays["consts"] = constants()
    return arrays


def kernel(**inputs):
    import concourse.bacc as bacc
    from concourse.bass_utils import run_bass_kernel_spmd

    nc = bacc.Bacc("TRN2", target_bir_lowering=False, num_devices=1, dynamic_dma_scratch_size=1024)
    arrays = layout(inputs)
    aps = {n: nc.dram_tensor(f"in_{n}", v.shape, F32, kind="ExternalInput").ap() for n, v in arrays.items()}
    out = nc.dram_tensor("out", (1, T, D), F32, kind="ExternalOutput").ap()
    build_program(nc, aps, out)
    r = run_bass_kernel_spmd(nc, [{f"in_{n}": v for n, v in arrays.items()}], core_ids=[0])
    return r.results[0]["out"]
```
